# Optimizing a Trainium2 kernel written in Bass

```python
import math
import jax
import jax.numpy as jnp
from jax import lax
import numpy as np

D_MODEL = 1024
BATCH = 1
SEQ = 256
DEPTH = 2

CTX_LEN = 256
GRID_W = 64
RMS_EPS = 1e-6
L2_EPS = 1e-6
ROPE_THETA = 10000.0
Q_BLOCK = 128

HEAD_DIM = 64
ATTN_SCALE = HEAD_DIM ** -0.5
DIFF_HEADS = 4
DIFF_V_DIM = 2 * HEAD_DIM
GQA_Q_HEADS = 8
GQA_KV_HEADS = 2
GQA_REP = GQA_Q_HEADS // GQA_KV_HEADS
DIFF_QK_W = DIFF_HEADS * 2 * HEAD_DIM
DIFF_V_W = DIFF_HEADS * DIFF_V_DIM
GQA_Q_W = GQA_Q_HEADS * HEAD_DIM
GQA_KV_W = GQA_KV_HEADS * HEAD_DIM
ATTN_SPLIT_IDX = (DIFF_QK_W, 2 * DIFF_QK_W, 2 * DIFF_QK_W + DIFF_V_W,
                  2 * DIFF_QK_W + DIFF_V_W + GQA_Q_W,
                  2 * DIFF_QK_W + DIFF_V_W + GQA_Q_W + GQA_KV_W)
ATTN_IN_W = 2 * DIFF_QK_W + DIFF_V_W + GQA_Q_W + 2 * GQA_KV_W
ATTN_OUT_W = DIFF_V_W + GQA_Q_W

GDN_HEADS = 8
GDN_HEAD_DIM = 128
GDN_W = GDN_HEADS * GDN_HEAD_DIM
GDN_CONV_K = 4
GDN_CONV_LEFT = 2
GDN_CHUNK = 64
GDN_IN_W = 4 * GDN_W + 4 * GDN_HEADS

FFN_HIDDEN = -(-8 * D_MODEL // (3 * 256)) * 256

kernel_name = "hybrid_diffgqa_gdeltanet_dit_prefix"

def rms_norm(x, g):
    xf = x.astype(jnp.float32)
    y = xf * lax.rsqrt(jnp.mean(xf * xf, axis=-1, keepdims=True) + RMS_EPS)
    return (y * g.astype(jnp.float32)).astype(x.dtype)

def l2_normalize(x):
    xf = x.astype(jnp.float32)
    return xf * lax.rsqrt(jnp.sum(xf * xf, axis=-1, keepdims=True) + L2_EPS)

def modulate(h, shift, scale):
    return h * (1.0 + scale) + shift

def axial_rope_tables(n_tokens, rows):
    row_ids = jnp.repeat(jnp.arange(rows, dtype=jnp.float32), GRID_W)[:n_tokens]
    col_ids = jnp.tile(jnp.arange(GRID_W, dtype=jnp.float32), rows)[:n_tokens]
    axis_dim = HEAD_DIM // 2
    inv_freq = ROPE_THETA ** (-jnp.arange(0, axis_dim, 2, dtype=jnp.float32) / axis_dim)
    ang_r = row_ids[:, None] * inv_freq
    ang_c = col_ids[:, None] * inv_freq
    ang = jnp.concatenate([ang_r, ang_r, ang_c, ang_c], axis=-1)
    return jnp.cos(ang), jnp.sin(ang)

def apply_axial_rope(x, cos, sin):
    shape = (1, cos.shape[0]) + (1,) * (x.ndim - 3) + (cos.shape[1],)
    cos = cos.reshape(shape).astype(x.dtype)
    sin = sin.reshape(shape).astype(x.dtype)
    x1, x2, x3, x4 = jnp.split(x, 4, axis=-1)
    rot = jnp.concatenate([-x2, x1, -x4, x3], axis=-1)
    return x * cos + rot * sin

def sweep_query_blocks(fn, *qs):
    B, L = qs[0].shape[:2]
    n_blk = L // Q_BLOCK
    blocks = tuple(jnp.swapaxes(q.reshape((B, n_blk, Q_BLOCK) + q.shape[2:]), 0, 1) for q in qs)
    out = lax.map(lambda blk: fn(*blk), blocks)
    return jnp.swapaxes(out, 0, 1).reshape((B, L) + out.shape[3:])

def attn_project(h, w_in, qk_g, rope):
    B, L, _ = h.shape
    p = h @ w_in
    dq, dk, dv, gq, gk, gv = jnp.split(p, ATTN_SPLIT_IDX, axis=-1)
    dq = dq.reshape(B, L, DIFF_HEADS, 2, HEAD_DIM)
    dk = dk.reshape(B, L, DIFF_HEADS, 2, HEAD_DIM)
    dv = dv.reshape(B, L, DIFF_HEADS, DIFF_V_DIM)
    gq = rms_norm(gq.reshape(B, L, GQA_KV_HEADS, GQA_REP, HEAD_DIM), qk_g[0])
    gk = rms_norm(gk.reshape(B, L, GQA_KV_HEADS, HEAD_DIM), qk_g[1])
    gv = gv.reshape(B, L, GQA_KV_HEADS, HEAD_DIM)
    if rope is not None:
        cos, sin = rope
        dq = apply_axial_rope(dq, cos, sin)
        dk = apply_axial_rope(dk, cos, sin)
        gq = apply_axial_rope(gq, cos, sin)
        gk = apply_axial_rope(gk, cos, sin)
    return dq, dk, dv, gq, gk, gv

def attend_heads(dq, gq, keys, lam, lam_init, subln_g):
    dk, dv, gk, gv = keys
    B, Q = dq.shape[:2]
    s = jnp.einsum('bqhmd,bthmd->bhmqt', dq, dk) * ATTN_SCALE
    p = jax.nn.softmax(s.astype(jnp.float32), axis=-1)
    a = (p[:, :, 0] - lam * p[:, :, 1]).astype(dv.dtype)
    d_out = jnp.einsum('bhqt,bthe->bqhe', a, dv)
    d_out = rms_norm(d_out, subln_g) * (1.0 - lam_init)
    s = jnp.einsum('bqgrd,btgd->bgrqt', gq, gk) * ATTN_SCALE
    p = jax.nn.softmax(s.astype(jnp.float32), axis=-1).astype(gv.dtype)
    g_out = jnp.einsum('bgrqt,btgd->bqgrd', p, gv)
    return jnp.concatenate([d_out.reshape(B, Q, DIFF_V_W), g_out.reshape(B, Q, GQA_Q_W)], axis=-1)

def even_mixer(h_lat, h_ctx, w_in, w_out, lam_vec, subln_g, qk_g, lam_init, rope, need_ctx):
    lv = lam_vec.astype(jnp.float32)
    lam = jnp.exp(jnp.sum(lv[0] * lv[1])) - jnp.exp(jnp.sum(lv[2] * lv[3])) + lam_init
    cq_d, ck_d, cv_d, cq_g, ck_g, cv_g = attn_project(h_ctx, w_in, qk_g, None)
    lq_d, lk_d, lv_d, lq_g, lk_g, lv_g = attn_project(h_lat, w_in, qk_g, rope)
    ctx_keys = (ck_d, cv_d, ck_g, cv_g)
    all_keys = tuple(jnp.concatenate([kc, kl], axis=1)
                     for kc, kl in zip(ctx_keys, (lk_d, lv_d, lk_g, lv_g)))
    o_lat = sweep_query_blocks(
        lambda dq, gq: attend_heads(dq, gq, all_keys, lam, lam_init, subln_g), lq_d, lq_g)
    y_lat = o_lat @ w_out
    y_ctx = None
    if need_ctx:
        y_ctx = attend_heads(cq_d, cq_g, ctx_keys, lam, lam_init, subln_g) @ w_out
    return y_lat, y_ctx

def short_conv(x, w):
    L = x.shape[1]
    xp = jnp.pad(x, ((0, 0), (GDN_CONV_LEFT, GDN_CONV_K - 1 - GDN_CONV_LEFT), (0, 0)))
    out = xp[:, 0:L] * w[0]
    for j in range(1, GDN_CONV_K):
        out = out + xp[:, j:j + L] * w[j]
    return out

def gdn_project(h, w_in, conv_w, a_log, dt_bias):
    B, L, _ = h.shape
    p = h @ w_in
    qkv, z, a, b = jnp.split(p, (3 * GDN_W, 4 * GDN_W, 4 * GDN_W + 2 * GDN_HEADS), axis=-1)
    qkv = jax.nn.silu(short_conv(qkv, conv_w))
    q, k, v = (t.reshape(B, L, GDN_HEADS, GDN_HEAD_DIM) for t in jnp.split(qkv, 3, axis=-1))
    q = l2_normalize(q) * (GDN_HEAD_DIM ** -0.5)
    k = l2_normalize(k)
    a = a.reshape(B, L, 2, GDN_HEADS).astype(jnp.float32)
    b = b.reshape(B, L, 2, GDN_HEADS).astype(jnp.float32)
    g = -jnp.exp(a_log.astype(jnp.float32)) * jax.nn.softplus(a + dt_bias.astype(jnp.float32))
    beta = jax.nn.sigmoid(b)
    return q, k, v, z.reshape(B, L, GDN_HEADS, GDN_HEAD_DIM), g, beta

def gated_delta_chunked(q, k, v, g, beta, state0):
    B, L, H, DK = q.shape
    DV = v.shape[-1]
    n = L // GDN_CHUNK
    f32 = jnp.float32

    def to_chunks(t):
        return jnp.transpose(t.astype(f32).reshape(B, n, GDN_CHUNK, H, t.shape[-1]), (1, 0, 3, 2, 4))

    qc, kc, vc = to_chunks(q), to_chunks(k), to_chunks(v)
    gc = jnp.transpose(g.astype(f32).reshape(B, n, GDN_CHUNK, H), (1, 0, 3, 2))
    bc = jnp.transpose(beta.astype(f32).reshape(B, n, GDN_CHUNK, H), (1, 0, 3, 2))
    gcum = jnp.cumsum(gc, axis=-1)
    tril = jnp.tril(jnp.ones((GDN_CHUNK, GDN_CHUNK), dtype=bool))
    strict = jnp.tril(jnp.ones((GDN_CHUNK, GDN_CHUNK), dtype=bool), -1)
    diff = gcum[..., :, None] - gcum[..., None, :]
    decay = jnp.where(tril, jnp.exp(jnp.where(tril, diff, 0.0)), 0.0)
    kb = kc * bc[..., None]
    vb = vc * bc[..., None]
    m = jnp.where(strict, jnp.einsum('nbhid,nbhjd->nbhij', kb, kc) * decay, 0.0)
    eye = jnp.eye(GDN_CHUNK, dtype=f32)
    tmat = lax.linalg.triangular_solve(eye + m, jnp.broadcast_to(eye, m.shape),
                                       left_side=True, lower=True, unit_diagonal=True)
    u = jnp.einsum('nbhij,nbhjd->nbhid', tmat, vb)
    w = jnp.einsum('nbhij,nbhjd->nbhid', tmat, kb * jnp.exp(gcum)[..., None])

    def step(S, xs):
        q_i, k_i, u_i, w_i, g_i, dec_i = xs
        attn = jnp.einsum('bhid,bhjd->bhij', q_i, k_i) * dec_i
        v_new = u_i - jnp.einsum('bhid,bhde->bhie', w_i, S)
        o = (jnp.einsum('bhid,bhde->bhie', q_i * jnp.exp(g_i)[..., None], S)
             + jnp.einsum('bhij,bhje->bhie', attn, v_new))
        g_last = g_i[..., -1]
        S = (S * jnp.exp(g_last)[..., None, None]
             + jnp.einsum('bhid,bhie->bhde', k_i * jnp.exp(g_last[..., None] - g_i)[..., None], v_new))
        return S, o

    S, o = lax.scan(step, state0.astype(f32), (qc, kc, u, w, gcum, decay))
    o = jnp.transpose(o, (1, 0, 3, 2, 4)).reshape(B, L, H, DV)
    return o.astype(v.dtype), S

def odd_mixer(h_lat, h_ctx, w_in, conv_w, a_log, dt_bias, norm_g, w_out, need_ctx):
    cq, ck, cv, cz, cg, cb = gdn_project(h_ctx, w_in, conv_w, a_log, dt_bias)
    lq, lk, lv, lz, lg, lb = gdn_project(h_lat, w_in, conv_w, a_log, dt_bias)
    B = h_lat.shape[0]
    s0 = jnp.zeros((B, GDN_HEADS, GDN_HEAD_DIM, GDN_HEAD_DIM), jnp.float32)
    flip = lambda t: jnp.flip(t, axis=1)
    o_cf, s_f = gated_delta_chunked(cq, ck, cv, cg[:, :, 0], cb[:, :, 0], s0)
    o_lf, _ = gated_delta_chunked(lq, lk, lv, lg[:, :, 0], lb[:, :, 0], s_f)
    o_cb, s_b = gated_delta_chunked(flip(cq), flip(ck), flip(cv), flip(cg[:, :, 1]), flip(cb[:, :, 1]), s0)
    o_lb, _ = gated_delta_chunked(flip(lq), flip(lk), flip(lv), flip(lg[:, :, 1]), flip(lb[:, :, 1]), s_b)

    def readout(o, z):
        o = rms_norm(o, norm_g) * jax.nn.silu(z)
        return o.reshape(o.shape[0], o.shape[1], GDN_W) @ w_out

    y_lat = readout(o_lf + flip(o_lb), lz)
    y_ctx = readout(o_cf + flip(o_cb), cz) if need_ctx else None
    return y_lat, y_ctx

def swiglu(h, w_gate_up, w_down):
    gate, up = jnp.split(h @ w_gate_up, 2, axis=-1)
    return (jax.nn.silu(gate) * up) @ w_down

def setup_inputs(seed: int = 0) -> dict:
    key = jax.random.key(seed)
    ks = jax.random.split(key, 20)
    f32 = jnp.float32
    n_even = (DEPTH + 1) // 2
    n_odd = DEPTH // 2

    def nrm(k, shape, scale):
        return jax.random.normal(k, shape, f32) * scale

    x = nrm(ks[0], (BATCH, SEQ, D_MODEL), 1.0)
    c = nrm(ks[1], (BATCH, D_MODEL), 1.0)
    ctx = nrm(ks[2], (BATCH, CTX_LEN, D_MODEL), 1.0)
    c_ctx = nrm(ks[3], (D_MODEL,), 1.0)
    ada_w = nrm(ks[4], (DEPTH, D_MODEL, 6 * D_MODEL), 0.5 * D_MODEL ** -0.5)
    ada_b = nrm(ks[5], (DEPTH, 6 * D_MODEL), 0.02)
    norm_g = 1.0 + nrm(ks[6], (DEPTH, 4, D_MODEL), 0.05)
    attn_w_in = nrm(ks[7], (n_even, D_MODEL, ATTN_IN_W), D_MODEL ** -0.5)
    attn_w_out = nrm(ks[8], (n_even, ATTN_OUT_W, D_MODEL), ATTN_OUT_W ** -0.5)
    diff_lambda = nrm(ks[9], (n_even, 4, HEAD_DIM), 0.1)
    diff_subln_g = 1.0 + nrm(ks[10], (n_even, DIFF_V_DIM), 0.05)
    gqa_qk_g = 1.0 + nrm(ks[11], (n_even, 2, HEAD_DIM), 0.05)
    gdn_w_in = nrm(ks[12], (n_odd, D_MODEL, GDN_IN_W), D_MODEL ** -0.5)
    gdn_conv_w = nrm(ks[13], (n_odd, GDN_CONV_K, 3 * GDN_W), GDN_CONV_K ** -0.5)
    gdn_a_log = jnp.log(jax.random.uniform(ks[14], (n_odd, 2, GDN_HEADS), f32, 1.0, 16.0))
    dt = jnp.exp(jax.random.uniform(ks[15], (n_odd, 2, GDN_HEADS), f32, math.log(1e-3), math.log(1e-1)))
    gdn_dt_bias = dt + jnp.log(-jnp.expm1(-dt))
    gdn_norm_g = 1.0 + nrm(ks[16], (n_odd, GDN_HEAD_DIM), 0.05)
    gdn_w_out = nrm(ks[17], (n_odd, GDN_W, D_MODEL), GDN_W ** -0.5)
    ffn_w_gate_up = nrm(ks[18], (DEPTH, D_MODEL, 2 * FFN_HIDDEN), D_MODEL ** -0.5)
    ffn_w_down = nrm(ks[19], (DEPTH, FFN_HIDDEN, D_MODEL), FFN_HIDDEN ** -0.5)
    return {"x": x, "c": c, "ctx": ctx, "c_ctx": c_ctx, "ada_w": ada_w, "ada_b": ada_b,
            "norm_g": norm_g, "attn_w_in": attn_w_in, "attn_w_out": attn_w_out,
            "diff_lambda": diff_lambda, "diff_subln_g": diff_subln_g, "gqa_qk_g": gqa_qk_g,
            "gdn_w_in": gdn_w_in, "gdn_conv_w": gdn_conv_w, "gdn_a_log": gdn_a_log,
            "gdn_dt_bias": gdn_dt_bias, "gdn_norm_g": gdn_norm_g, "gdn_w_out": gdn_w_out,
            "ffn_w_gate_up": ffn_w_gate_up, "ffn_w_down": ffn_w_down}

def reference(x, c, ctx, c_ctx, ada_w, ada_b, norm_g, attn_w_in, attn_w_out, diff_lambda,
              diff_subln_g, gqa_qk_g, gdn_w_in, gdn_conv_w, gdn_a_log, gdn_dt_bias, gdn_norm_g,
              gdn_w_out, ffn_w_gate_up, ffn_w_down):
    n_tokens = x.shape[1]
    rows = n_tokens // GRID_W
    rope = axial_rope_tables(n_tokens, rows)
    x_ctx = ctx
    silu_c = jax.nn.silu(c)
    silu_cc = jax.nn.silu(c_ctx)
    for l in range(DEPTH):
        need_ctx = l < DEPTH - 1
        i = l // 2
        mod_lat = (silu_c @ ada_w[l] + ada_b[l])[:, None, :]
        mod_ctx = silu_cc @ ada_w[l] + ada_b[l]
        sh1, sc1, gt1, sh2, sc2, gt2 = jnp.split(mod_lat, 6, axis=-1)
        csh1, csc1, cgt1, csh2, csc2, cgt2 = jnp.split(mod_ctx, 6, axis=-1)
        h_lat = modulate(rms_norm(x, norm_g[l, 0]), sh1, sc1)
        h_ctx = modulate(rms_norm(x_ctx, norm_g[l, 0]), csh1, csc1)
        if l % 2 == 0:
            lam_init = 0.8 - 0.6 * math.exp(-0.3 * l)
            y_lat, y_ctx = even_mixer(h_lat, h_ctx, attn_w_in[i], attn_w_out[i], diff_lambda[i],
                                      diff_subln_g[i], gqa_qk_g[i], lam_init, rope, need_ctx)
        else:
            y_lat, y_ctx = odd_mixer(h_lat, h_ctx, gdn_w_in[i], gdn_conv_w[i], gdn_a_log[i],
                                     gdn_dt_bias[i], gdn_norm_g[i], gdn_w_out[i], need_ctx)
        x = x + gt1 * rms_norm(y_lat, norm_g[l, 1])
        h = modulate(rms_norm(x, norm_g[l, 2]), sh2, sc2)
        x = x + gt2 * rms_norm(swiglu(h, ffn_w_gate_up[l], ffn_w_down[l]), norm_g[l, 3])
        if need_ctx:
            x_ctx = x_ctx + cgt1 * rms_norm(y_ctx, norm_g[l, 1])
            hc = modulate(rms_norm(x_ctx, norm_g[l, 2]), csh2, csc2)
            x_ctx = x_ctx + cgt2 * rms_norm(swiglu(hc, ffn_w_gate_up[l], ffn_w_down[l]), norm_g[l, 3])
    return x


_drawn_inputs = setup_inputs


def setup_inputs(seed=0):
    import zlib

    import numpy as np

    out = dict(_drawn_inputs(seed))
    spreads = {}
    factors = {'diff_lambda': 8.0, 'diff_subln_g': 3.35, 'gqa_qk_g': 8.0, 'gdn_norm_g': 3.917}
    for name, (base, spread) in spreads.items():
        noise = np.random.default_rng([zlib.crc32(name.encode()), seed]).standard_normal(out[name].shape)
        drawn = base * np.exp(spread * noise) if base else spread * noise
        out[name] = jnp.asarray(drawn.astype(out[name].dtype))
    for name, factor in factors.items():
        out[name] = (out[name] * factor).astype(out[name].dtype)
    return out
```

```python
from contextlib import ExitStack

import numpy as np

import concourse.bass as bass
from concourse import mybir

F32 = mybir.dt.float32
F32R = mybir.dt.float32r
BF16 = mybir.dt.bfloat16
ALU = mybir.AluOpType
ACT = mybir.ActivationFunctionType
AXIS_X = mybir.AxisListType.X

P = 128
D = 1024
KT = D // P
CTX, LAT = 256, 256
T = CTX + LAT
STREAMS = ((0, CTX), (CTX, T))
GRID_W = 64
ROPE_THETA = 10000.0
RMS_EPS = 1e-6
HEAD = 64
DIFF_HEADS = 4
GQA_HEADS = 8
GQA_KV = 2
DQ_COL, DK_COL, DV_COL, GQ_COL, GK_COL, GV_COL = 0, 512, 1024, 1536, 2048, 2176
LAM_INIT = 0.8 - 0.6 * 1.0
GDN_SCALE = 128 ** -0.5
FFN = 2816
FT = FFN // P
GH = 8
GW = GH * P
CHUNK = 128
LEVELS = 7

C_IDENT, C_ONES, C_BLOCK, C_ROT = 0, 128, 256, 384
C_COS, C_SIN = 512, 768
C_TRIF, C_TRIB = 1024, 1152
C_HALF = 1280
C_EPS = 1282
C_ONE = 1283
C_N = 1284

R_NORM, R_C, R_SUB, R_GDN, R_QKG, R_N = 0, 64, 80, 81, 82, 84


def shape_tables():
    t = np.zeros((P, C_N), np.float32)
    i = np.arange(P)
    t[i, C_IDENT + i] = 1
    t[:, C_ONES:C_ONES + P] = 1
    t[:, C_BLOCK:C_BLOCK + P] = (i[:, None] // HEAD == i[None, :] // HEAD)
    q = (i % 32) // 16
    low, high = i[q == 0], i[q == 1]
    t[low + 16, C_ROT + low] = -1
    t[high - 16, C_ROT + high] = 1
    n = np.arange(LAT)
    freq = ROPE_THETA ** (-np.arange(0, HEAD // 2, 2, dtype=np.float32) / np.float32(HEAD // 2))
    rows, cols = (n // GRID_W).astype(np.float32), (n % GRID_W).astype(np.float32)
    d = i % HEAD
    ang = np.where((d < HEAD // 2)[:, None], rows[None, :], cols[None, :]) * freq[d % 16][:, None]
    t[:, C_COS:C_COS + LAT] = np.cos(ang)
    t[:, C_SIN:C_SIN + LAT] = np.sin(ang)
    t[:, C_TRIF:C_TRIF + P] = (i[:, None] <= i[None, :])
    t[:, C_TRIB:C_TRIB + P] = (i[:, None] >= i[None, :])
    t[:HEAD, C_HALF] = HEAD ** -0.5
    t[HEAD:, C_HALF + 1] = HEAD ** -0.5
    t[:, C_EPS] = RMS_EPS
    t[:, C_ONE] = 1
    return t


def level_tables():
    i = np.arange(P)
    m = np.zeros((P, LEVELS, 3, P), np.float32)
    for n in range(LEVELS):
        s = 1 << n
        row, col = i[:, None], i[None, :]
        low = (row // (2 * s) == col // (2 * s)) & (row // s % 2 == 1) & (col // s % 2 == 0)
        m[:, n, 0], m[:, n, 1], m[:, n, 2] = low, low.T, low
    return m.reshape(P, LEVELS * 3 * P)


QKV_STEPS = ([("gk", 0), ("gv", 0)] + [("dk", t) for t in range(4)] + [("dv", t) for t in range(4)]
             + [("dq", t) for t in range(4)] + [("gq", t) for t in range(4)])
ATT_UNITS = [(head, qb) for head in range(DIFF_HEADS + GQA_HEADS) for qb in range(T // P)]
QK_TILES = [s for s in QKV_STEPS if s[0] not in ("gv", "dv")]
NORMED = [u for u, s in enumerate(QK_TILES) if s[0] in ("gk", "gq")]
GDN_STEPS = ([("ab", 0)] + [("k", h) for h in range(GH)] + [("v", h) for h in range(GH)]
             + [("q", h) for h in range(GH)] + [("z", h) for h in range(GH)])
CONV_TILES = [s for s in GDN_STEPS if s[0] in "kvq"]
CONV_CHANNEL = {"q": 0, "k": GH, "v": 2 * GH}
DOWN_PARTS = ((0, 8), (8, 16), (16, FT))


def stat_at(n):
    return [u for u in NORMED if QKV_STEPS.index(QK_TILES[u]) == n - 1]


def rotate_at(n):
    return [u for u, s in enumerate(QK_TILES) if QKV_STEPS.index(s) == n - (2 if u in NORMED else 1)]


def maps_of(head):
    if head < DIFF_HEADS:
        return [(head, 0, 1 + head), (head, 1, 1 + head)]
    g, r = divmod(head - DIFF_HEADS, GQA_HEADS // GQA_KV)
    return [(DIFF_HEADS + r, g, 0)]


def map_no(n, m):
    pairs = min(n, DIFF_HEADS * 4)
    return n + pairs + m


def keys_of(qb):
    return T if qb >= CTX // P else CTX


def scan_chunk(d, step):
    return step if d == 0 else (1, 0, 3, 2)[step]


def ada_after(phase, step):
    if phase == "start":
        return list(range(16))
    if phase == "qkv":
        return [16 + step]
    if phase == "att" and step % 3 == 2 and step // 3 < 14:
        return [34 + step // 3]
    if phase == "gate0":
        return [48 + step]
    if phase == "down0" and 0 <= step < 4:
        return [92 + step]
    return []


def stream():
    out = [("ada", n) for n in ada_after("start", 0)]
    for n, (kind, t) in enumerate(QKV_STEPS):
        out += [("qkv", kind, t)] + [("ada", a) for a in ada_after("qkv", n)]
    for n in range(len(ATT_UNITS)):
        out += [("ada", a) for a in ada_after("att", n)]
    out += [("attout", m) for m in range(KT)]
    for layer in range(2):
        if layer:
            out += [("gdn", kind, t) for kind, t in GDN_STEPS] + [("gdnout", m) for m in range(KT)]
        for n in range(2 * FT):
            out += [("gate", layer, n)] + [("ada", a) for a in ada_after(f"gate{layer}", n)]
        for m in range(KT):
            out += [("down", layer, m, part) for part in range(3)]
            out += [("ada", a) for a in ada_after(f"down{layer}", m)]
    return out


def backbone(nc, x, c, ctx, c_ctx, ada_w, ada_b, norm_g, attn_w_in, attn_w_out, diff_lambda,
             diff_subln_g, gqa_qk_g, gdn_w_in, gdn_conv_w, gdn_a_log, gdn_dt_bias, gdn_norm_g,
             gdn_w_out, ffn_w_gate_up, ffn_w_down, tables, levels, out):
    with ExitStack() as stack:
        def sem(name):
            return stack.enter_context(nc.semaphore(name))

        top = [(nc.sbuf_base + 31) // 32 * 32]

        def at(name, shape, dtype, offset):
            return nc.alloc_sbuf_tensor_at(name, [P] + shape, dtype, offset=offset)[:]

        def place(name, shape, dtype=F32):
            size = int(np.prod(shape)) * (2 if dtype == BF16 else 4)
            offset = top[0]
            top[0] += (size + 31) // 32 * 32
            return at(name, shape, dtype, offset)

        N_RAW, N_SPLIT = 5, 3
        xT = place("xT", [KT, T])
        H_BASE = top[0]
        h_hi = place("h_hi", [KT, T], F32R)
        h_lo = place("h_lo", [KT, T], F32R)
        w_raw = [place(f"w_raw{n}", [KT, P]) for n in range(N_RAW)]
        w_hi = [place(f"w_hi{n}", [KT, P], F32R) for n in range(N_SPLIT)]
        w_lo = [place(f"w_lo{n}", [KT, P], F32R) for n in range(N_SPLIT)]
        BIG = top[0]
        top[0] += FT * T * 4 * 2
        scr = top[0]
        top[0] += 8448
        tab = place("tab", [C_N])
        level_mask = place("level_mask", [LEVELS, 3, P], BF16)
        colsA = place("colsA", [R_N])
        ada_bias = place("ada_bias", [2 * 6 * KT])
        conv_cols = place("conv_cols", [4 * 3 * GH])
        silu_c = place("silu_c", [KT, 2])
        mods = place("mods", [2, 6, KT, 2])
        lam_row = place("lam_row", [4 * HEAD])
        lam_two = place("lam_two", [5])
        dt_row = place("dt_row", [2 * GH])
        alog_row = place("alog_row", [2 * GH])
        gates = place("gates", [10, 4, 2 * GH])
        stats = place("stats", [4, 6])
        sub_gain = place("sub_gain", [1])
        el = place("el", [4, 4])
        wl = place("wl", [4, 4])
        assert top[0] <= nc.sbuf_usable_end, (top[0], nc.sbuf_usable_end)

        ident, ones = tab[:, C_IDENT:C_IDENT + P], tab[:, C_ONES:C_ONES + P]
        block_ones, rotation = tab[:, C_BLOCK:C_BLOCK + P], tab[:, C_ROT:C_ROT + P]
        cosT, sinT = tab[:, C_COS:C_COS + LAT], tab[:, C_SIN:C_SIN + LAT]
        tri = [tab[:, C_TRIF:C_TRIF + P], tab[:, C_TRIB:C_TRIB + P]]
        eps, one = tab[:, C_EPS:C_EPS + 1], tab[:, C_ONE:C_ONE + 1]

        tok = at("tok", [4, D], F32, BIG)
        rowsA = at("rowsA", [P], F32, BIG + 16384)
        rowsB = at("rowsB", [P], F32, BIG + 16896)
        rowsC = at("rowsC", [P], F32, BIG + 17408)
        level_f32 = at("level_f32", [LEVELS * 3 * P], F32, BIG + 18432)
        act_hi = at("act_hi", [FT, T], F32R, BIG)
        act_lo = at("act_lo", [FT, T], F32R, BIG + FT * T * 4)
        q_sb = at("q_sb", [KT, 2, T], F32, BIG)
        k_sb = at("k_sb", [5, T], F32, BIG + 32768)
        v_sb = at("v_sb", [4, 768], F32, BIG + 43008)
        probs = at("probs", [3, 2, T], F32, BIG + 55296)
        probsT = at("probsT", [2, 4, P], F32, BIG + 67584)
        o_sb = at("o_sb", [KT, T], F32, BIG + 71680)
        o_sq = at("o_sq", [T], F32, BIG + 88064)
        qk_n = at("qk_n", [3, T], F32, BIG + 71680)
        qk_sq = at("qk_sq", [2, T], F32, BIG + 77824)
        qk_cosed = at("qk_cosed", [2, LAT], F32, BIG + 81920)
        qk_sined = at("qk_sined", [2, LAT], F32, BIG + 83968)
        s_tmp = at("s_tmp", [2, T], F32, scr)
        a_tmp = at("a_tmp", [2, T], F32, scr + 4096)

        k_fm = at("k_fm", [GH, T], F32, BIG)
        k_tok = at("k_tok", [4, GH, P], F32, BIG + 16384)
        v_tok = at("v_tok", [4, GH, P], F32, BIG + 32768)
        q_fm = at("q_fm", [GH, LAT], F32, BIG + 49152)
        z_fm = at("z_fm", [GH, LAT], F32, BIG + 57344)
        o_fm = at("o_fm", [GH, LAT], F32, BIG + 65536)
        u_beta = at("u_beta", [4, 4, P], F32, BIG + 73728)
        attnT = at("attnT", [2, 4, P], F32, BIG + 81920)
        q_dec = at("q_dec", [2, 4, P], F32, BIG + 86016)
        gdn_sq = at("gdn_sq", [2, T], F32, BIG + 73728)
        read_t = at("read_t", [2, LAT], F32, BIG + 77824)
        conv_in = [at(f"conv_in{n}", [2, CTX + 3], F32, scr + 2080 * n) for n in range(2)]
        conv_out = [at(f"conv_out{n}", [T], F32, scr + 4160 + 2048 * n) for n in range(2)]
        masked_v = at("masked_v", [2, 4, P], F32, scr)
        masked_w = at("masked_w", [2, 4, P], F32, scr + 4096)
        row_decay = at("row_decay", [2, 4, P], F32, scr)
        h_area = [[at(f"h_area{n}_{m}", [4, P], F32, H_BASE + 8192 * n + 2048 * m) for m in range(4)]
                  for n in range(4)]
        n_mat = [h_area[c][0] for c in range(4)]
        t_mat = [h_area[c][1] for c in range(4)]
        u_mat = [h_area[c][2] for c in range(4)]
        z_mat = [h_area[c][3] for c in range(4)]
        state, scan_rhs, v_new, v_end = h_area[0]

        def norm_views(name, offset):
            return (at(name + "_rstd", [T], F32, offset), at(name + "_t", [2, T], F32, offset + 2048),
                    at(name + "_sq", [2, T], F32, offset + 6144),
                    at(name + "_acc", [T], F32, offset + 10240))

        pre_rstd, pre_t, pre_sq, _ = norm_views("pre", BIG + 73728)
        pre_h = at("pre_h", [2, T], F32, BIG + 73728 + 12288)
        post_views = [norm_views("post0", BIG + 73728), norm_views("post1", H_BASE + 16384),
                      norm_views("post2", BIG + 73728), norm_views("post3", H_BASE + 16384)]
        y_views = [at("y0", [KT, T], F32, BIG), at("y1", [KT, T], F32, H_BASE),
                   at("y2", [KT, T], F32, BIG), at("y3", [KT, T], F32, H_BASE)]
        out_sb = at("out_sb", [2, D], F32, BIG)

        banks = [stack.enter_context(nc.psum_tensor(f"bank{n}", [P, T], F32))[:] for n in range(8)]
        RINGS = {"work": (2, 3, 4, 5, 6), "side": (7, 1)}
        taken = {"work": 0, "side": 0}
        used = [0] * 8
        turn_of = {}
        done_at = {}

        products_done = sem("products_done")
        evacuated = [sem(f"evacuated{n}") for n in range(8)]
        raw_in = [sem(f"raw_in{n}") for n in range(N_RAW)]
        w_hi_ready, w_lo_ready = sem("w_hi_ready"), sem("w_lo_ready")
        tables_in, rows_in, tok_in = sem("tables_in"), sem("rows_in"), sem("tok_in")
        levels_in, levels_ready = sem("levels_in"), sem("levels_ready")
        act_chain, dve_chain, pool_chain = sem("act_chain"), sem("dve_chain"), sem("pool_chain")
        silu_ready = sem("silu_ready")
        lam_sums, lam_exps, lam_ready = sem("lam_sums"), sem("lam_exps"), sem("lam_ready")
        ada_taken, mods_ready = sem("ada_taken"), sem("mods_ready")
        pre_sq_ready, pre_t_ready = sem("pre_sq_ready"), sem("pre_t_ready")
        h32_ready, h_ready = sem("h32_ready"), sem("h_ready")
        y_acc_ready, post_t_ready, x_updated = sem("y_acc_ready"), sem("post_t_ready"), sem("x_updated")
        qk_normed, qk_cos, qk_roped, qk_out = sem("qk_normed"), sem("qk_cos"), sem("qk_roped"), sem("qk_out")
        max_ready, probs_ready, o_scaled = sem("max_ready"), sem("probs_ready"), sem("o_scaled")
        o_hi_ready, o_lo_ready = sem("o_hi_ready"), sem("o_lo_ready")
        act_hi_ready, act_lo_ready = sem("act_hi_ready"), sem("act_lo_ready")
        pads_ready = sem("pads_ready")
        conv_done, conv_silu = sem("conv_done"), sem("conv_silu")
        gate_pre, gate_exp, gate_sp, gate_ready = sem("gate_pre"), sem("gate_exp"), sem("gate_sp"), sem("gate_ready")
        gate_cum, gate_decay = sem("gate_cum"), sem("gate_decay")
        norm_sq, normed = sem("norm_sq"), sem("normed")
        tri_gates, diffs_ready = sem("tri_gates"), sem("diffs_ready")
        attn_raw, attn_ready, t_ready, u_ready, ub_ready = (sem("attn_raw"), sem("attn_ready"), sem("t_ready"),
                                                            sem("u_ready"), sem("ub_ready"))
        q_dec_ready, t_masked = sem("q_dec_ready"), sem("t_masked")
        rhs_ready, v_end_ready = sem("rhs_ready"), sem("v_end_ready")
        read_sq, read32 = sem("read_sq"), sem("read32")
        out_stored = sem("out_stored")

        chunks = stream()
        if LAST_SUB < 2:
            chunks = [k for k in chunks if k[0] == "ada" or k[0] in ("qkv", "attout") or k[1] == 0]
        where = {key: n for n, key in enumerate(chunks)}
        split_keys = [key for key in chunks if key[0] != "ada"]
        split_no = {key: n for n, key in enumerate(split_keys)}
        FIRST_CHUNK = [("qkv", "gk", 0), ("gate", 0, 0), ("gdn", "ab", 0), ("gate", 1, 0)]

        landed = []
        for n, key in enumerate(chunks):
            landed.append((landed[n - N_RAW] if n >= N_RAW else 0) + 16 * (2 if key[:2] == ("qkv", "gq") else 1))

        def raw_slot(key):
            return w_raw[where[key] % N_RAW]

        def wait_raw(eng, key):
            eng.wait_ge(raw_in[where[key] % N_RAW], landed[where[key]])

        def wait_product(eng, job):
            eng.wait_ge(products_done, done_at[job])

        def wait_evacuated(eng, job):
            bank, turn = turn_of[job]
            eng.wait_ge(evacuated[bank], turn)

        def release(ins, job):
            ins.then_inc(evacuated[turn_of[job][0]], 1)

        def bank(job):
            return banks[turn_of[job][0]]

        def chunk_width(key):
            return 2 * 2 * GH if key[:2] == ("gdn", "ab") else P

        def mod_col(layer, part, k, s):
            return mods[:, layer, part, k, s:s + 1]

        def first_token(i):
            return 0 if i < 3 else CTX

        def first_out(i):
            return 0 if i < 2 else CTX

        def x_ready(eng, i, k):
            if i == 0:
                wait_evacuated(eng, ("x", k))
            else:
                eng.wait_ge(x_updated, (i - 1) * KT + k + 1)

        def units(ap):
            return ap.rearrange("p (u n) -> p u n", n=P)

        def both(ap):
            return ap.unsqueeze(2).to_broadcast([P, 2, 2, P])

        HEAD_PAIRS = GH // 2
        CHUNKS = T // CHUNK
        LAT_CHUNK = CTX // CHUNK
        CONV_LAG = 2

        def conv_step(n):
            return CONV_TILES.index(GDN_STEPS[n]) if 0 <= n < len(GDN_STEPS) and GDN_STEPS[n] in CONV_TILES else None

        def conv_lo(u):
            return CTX if CONV_TILES[u][0] == "q" else 0

        def norm_tile(e):
            return (k_fm[:, e, :], T) if e < GH else (q_fm[:, e - GH, :], LAT)

        def gate_cols(ap, c, unit, p):
            col = unit // 2 * GH + 2 * p + unit % 2
            return ap[:, c, col:col + 1]

        log_decay, beta_g, cum_g, neg_decay = gates[:, 3], gates[:, 5], gates[:, 6], gates[:, 7]

        def end_col(d):
            return CHUNK - 1 if d == 0 else 0

        def build_no(p, level, c):
            return (p * LEVELS + level) * CHUNKS + c

        def gdn_tensor(pe, take, finish, project, project_tokens):
            for n in range(len(GDN_STEPS) + 1):
                u = conv_step(n - CONV_LAG)
                if u is not None and CONV_TILES[u][0] == "v":
                    pe.wait_ge(conv_silu, u + 1)
                    h = CONV_TILES[u][1]
                    dst = take(("vt", h))
                    for c in range(CHUNKS):
                        m = nc.tensor.transpose(dst[:, c * P:(c + 1) * P], conv_out[u % 2][:, c * P:(c + 1) * P], ident)
                    finish(m, ("vt", h))
                if n == len(GDN_STEPS):
                    break
                kind, h = GDN_STEPS[n]
                key = ("gdn", kind, h)
                if kind == "ab":
                    project_tokens(key, key, 4 * GH, 2)
                else:
                    project(key, key, CTX if kind in "qz" else 0)
                if n == 4:
                    pe.wait_ge(gate_sp, 1)
                    dst = take(("cum", 0), "side")
                    for c in range(CHUNKS):
                        for d in range(2):
                            a = c * 2 * GH + d * GH
                            m = nc.tensor.matmul(dst[:, a:a + GH], tri[d], log_decay[:, c, d * GH:(d + 1) * GH],
                                                 start=True, stop=True)
                    finish(m, ("cum", 0))

            for e in range(2 * GH + 2):
                if e < 2 * GH:
                    pe.wait_ge(norm_sq, e + 1)
                    width = norm_tile(e)[1]
                    dst = take(("ksum", e), "side")
                    finish(nc.tensor.matmul(dst[:, 0:width], ones, gdn_sq[:, e % 2, 0:width], start=True, stop=True),
                           ("ksum", e))
                if 2 <= e < GH + 2:
                    pe.wait_ge(normed, e - 1)
                    dst = take(("kt", e - 2))
                    for c in range(CHUNKS):
                        m = nc.tensor.transpose(dst[:, c * P:(c + 1) * P], k_fm[:, e - 2, c * P:(c + 1) * P], ident)
                    finish(m, ("kt", e - 2))

            for p in range(HEAD_PAIRS):
                for c in range(CHUNKS):
                    span = slice(c * CHUNK, (c + 1) * CHUNK)
                    pe.wait_ge(tri_gates, p * CHUNKS + c + 1)
                    finish(nc.tensor.matmul(take(("R", p, c), "side"), ones, n_mat[c].rearrange("p u n -> p (u n)"),
                                            start=True, stop=True), ("R", p, c))
                    if p == 0 and c == 0:
                        pe.wait_ge(normed, 2 * GH)
                    dst = take(("G", p, c))
                    for hh in range(2):
                        k_c = k_fm[:, 2 * p + hh, span]
                        m = nc.tensor.matmul(dst[:, hh * P:(hh + 1) * P], k_c, k_c, start=True, stop=True)
                    if c >= LAT_CHUNK:
                        for hh in range(2):
                            lat = slice((c - LAT_CHUNK) * CHUNK, (c - LAT_CHUNK + 1) * CHUNK)
                            m = nc.tensor.matmul(dst[:, (2 + hh) * P:(3 + hh) * P], k_fm[:, 2 * p + hh, span],
                                                 q_fm[:, 2 * p + hh, lat], start=True, stop=True)
                    finish(m, ("G", p, c))
                for c in range(CHUNKS):
                    wait_evacuated(pe, ("G", p, c))
                    dst = take(("NT", p, c))
                    for unit in range(4):
                        m = nc.tensor.transpose(dst[:, unit * P:(unit + 1) * P], n_mat[c][:, unit, :], ident)
                    finish(m, ("NT", p, c))
                for level in range(1, LEVELS):
                    for c in range(CHUNKS):
                        pe.wait_ge(u_ready, build_no(p, level - 1, c) + 1)
                        dst = take(("Z", p, level, c))
                        for unit in range(4):
                            m = nc.tensor.matmul(dst[:, unit * P:(unit + 1) * P], n_mat[c][:, unit, :],
                                                 u_mat[c][:, unit, :], start=True, stop=True)
                        finish(m, ("Z", p, level, c))
                    for c in range(CHUNKS):
                        wait_evacuated(pe, ("Z", p, level, c))
                        pe.wait_ge(t_ready, p * (LEVELS - 1) * CHUNKS + (level - 1) * CHUNKS + c + 1)
                        if level < LEVELS - 1:
                            dst = take(("V", p, level, c))
                            for unit in range(4):
                                m = nc.tensor.matmul(dst[:, unit * P:(unit + 1) * P], z_mat[c][:, unit, :],
                                                     t_mat[c][:, unit, :], start=True, stop=True)
                            finish(m, ("V", p, level, c))
                        dst = take(("W", p, level, c))
                        for unit in range(4):
                            m = nc.tensor.matmul(dst[:, unit * P:(unit + 1) * P], t_mat[c][:, unit, :],
                                                 z_mat[c][:, unit, :], start=True, stop=True)
                        finish(m, ("W", p, level, c))
                for s in range(CHUNKS):
                    cc = [scan_chunk(unit // 2, s) for unit in range(4)]
                    if s:
                        wait_evacuated(pe, ("S", p, s - 1))
                        dst = take(("KS", p, s))
                        for unit in range(4):
                            m = nc.tensor.matmul(dst[:, unit * P:(unit + 1) * P],
                                                 k_fm[:, 2 * p + unit % 2, cc[unit] * CHUNK:(cc[unit] + 1) * CHUNK],
                                                 state[:, unit, :], start=True, stop=True)
                        finish(m, ("KS", p, s))
                        wait_evacuated(pe, ("KS", p, s))
                    else:
                        pe.wait_ge(ub_ready, (p + 1) * CHUNKS)
                    dst = take(("VN", p, s))
                    for unit in range(4):
                        rhs = scan_rhs[:, unit, :] if s else v_tok[:, cc[unit], 2 * p + unit % 2, :]
                        m = nc.tensor.matmul(dst[:, unit * P:(unit + 1) * P], u_beta[:, cc[unit], unit, :], rhs,
                                             start=True, stop=True)
                    finish(m, ("VN", p, s))
                    if s < CHUNKS - 1:
                        pe.wait_ge(v_end_ready, p * (CHUNKS - 1) + s + 1)
                        dst = take(("S", p, s))
                        for unit in range(4):
                            m = nc.tensor.matmul(dst[:, unit * P:(unit + 1) * P],
                                                 k_tok[:, cc[unit], 2 * p + unit % 2, :], v_end[:, unit, :],
                                                 start=True, stop=True)
                        finish(m, ("S", p, s))
                    if s >= LAT_CHUNK:
                        wait_evacuated(pe, ("VN", p, s))
                        pe.wait_ge(attn_ready, (p + 1) * (CHUNKS - LAT_CHUNK))
                        dst = take(("O", p, s))
                        for unit in range(4):
                            part = dst[:, unit * P:(unit + 1) * P]
                            nc.tensor.matmul(part, state[:, unit, :], q_dec[:, cc[unit] - LAT_CHUNK, unit, :],
                                             start=True, stop=False)
                            m = nc.tensor.matmul(part, v_new[:, unit, :], attnT[:, cc[unit] - LAT_CHUNK, unit, :],
                                                 start=False, stop=True)
                        finish(m, ("O", p, s))
            for h in range(GH):
                pe.wait_ge(read_sq, h + 1)
                finish(nc.tensor.matmul(take(("osum", h), "side")[:, 0:LAT], ones, gdn_sq[:, h % 2, 0:LAT],
                                        start=True, stop=True), ("osum", h))

        def gdn_scalar(act, link, split_to, rstd):
            act.wait_ge(pads_ready, 1)
            for n in range(len(GDN_STEPS) + 1):
                if n < len(GDN_STEPS):
                    kind, h = GDN_STEPS[n]
                    key = ("gdn", kind, h)
                    split_to(split_no[key] + 2)
                    wait_product(act, key)
                    if kind == "ab":
                        act.wait_ge(gate_pre, 1)
                        b = bank(key)[:, 0:16 * GH].rearrange("p (c n) -> p c n", c=CHUNKS)[:, :, 2 * GH:4 * GH]
                        release(nc.scalar.activation(beta_g, b, ACT.Sigmoid), key)
                        link(nc.scalar.activation(gates[:, 2], gates[:, 2], ACT.Exp))
                        nc.scalar.activation(alog_row, alog_row, ACT.Exp)
                        nc.scalar.activation(gates[:, 2], gates[:, 2], ACT.Ln, bias=one).then_inc(gate_exp, 1)
                    elif kind == "z":
                        release(nc.scalar.activation(z_fm[:, h, :], bank(key)[:, CTX:T], ACT.Silu), key)
                    else:
                        u = CONV_TILES.index((kind, h))
                        if u >= 2:
                            act.wait_ge(conv_done, u - 1)
                        lo = conv_lo(u)
                        release(nc.scalar.activation(conv_in[u % 2][:, lo // CTX:2, 2:2 + CTX],
                                                     bank(key)[:, lo:T].rearrange("p (s n) -> p s n", n=CTX),
                                                     ACT.Copy), key)
                u = conv_step(n - 1)
                if u is not None:
                    act.wait_ge(conv_done, u + 1)
                    kind, h = CONV_TILES[u]
                    dst = {"k": k_fm[:, h, :], "q": q_fm[:, h, :], "v": conv_out[u % 2]}[kind]
                    nc.scalar.activation(dst, conv_out[u % 2][:, conv_lo(u):T], ACT.Silu).then_inc(conv_silu, 1)
                if n == 6:
                    wait_evacuated(act, ("cum", 0))
                    nc.scalar.activation(neg_decay, cum_g, ACT.Exp).then_inc(gate_decay, 1)

            def square(e):
                tile, width = norm_tile(e)
                if e >= 2:
                    act.wait_ge(normed, e - 1)
                act.wait_ge(conv_silu, len(CONV_TILES))
                nc.scalar.activation(gdn_sq[:, e % 2, 0:width], tile, ACT.Square).then_inc(norm_sq, 1)

            square(0)
            for e in range(2 * GH + 2):
                if e + 1 < 2 * GH:
                    square(e + 1)
                if e < 2 * GH:
                    width = norm_tile(e)[1]
                    rstd(gdn_sq[:, e % 2, 0:width], bank(("ksum", e))[:, 0:width], ("ksum", e), 1.0)
                if 2 <= e < GH + 2:
                    wait_product(act, ("kt", e - 2))
                    release(nc.scalar.activation(k_tok[:, :, e - 2, :], units(bank(("kt", e - 2))), ACT.Copy),
                            ("kt", e - 2))

            for p in range(HEAD_PAIRS):
                for c in range(CHUNKS):
                    act.wait_ge(diffs_ready, p * CHUNKS + c + 1)
                    nc.scalar.activation(t_mat[c], t_mat[c], ACT.Exp, scale=-1.0)
                    nc.scalar.activation(u_mat[c], u_mat[c], ACT.Exp)
                    rows = units(bank(("R", p, c)))
                    if c >= LAT_CHUNK:
                        nc.scalar.activation(row_decay[:, c - LAT_CHUNK], rows, ACT.Exp)
                    for d in range(2):
                        last = nc.scalar.activation(el[:, c, 2 * d:2 * d + 2],
                                                    rows[:, 2 * d:2 * d + 2, end_col(d)], ACT.Exp)
                    release(last, ("R", p, c))
                for level in range(1, LEVELS):
                    for c in range(CHUNKS):
                        job = ("Z", p, level, c)
                        wait_product(act, job)
                        if level > 1:
                            wait_product(act, ("W", p, level - 1, c))
                        release(nc.scalar.activation(z_mat[c], units(bank(job)), ACT.Copy), job)
                for c in range(CHUNKS):
                    act.wait_ge(u_ready, build_no(p, LEVELS - 1, c) + 1)
                    for unit in range(4):
                        last = nc.scalar.activation(u_beta[:, c, unit, :], u_mat[c][:, unit, :], ACT.Copy,
                                                    scale=gate_cols(beta_g, c, unit, p))
                    last.then_inc(ub_ready, 1)
                for s in range(CHUNKS):
                    wait_product(act, ("VN", p, s))
                    if s > LAT_CHUNK:
                        wait_product(act, ("O", p, s - 1))
                    if s:
                        act.wait_ge(v_end_ready, p * (CHUNKS - 1) + s)
                    release(nc.scalar.activation(v_new, units(bank(("VN", p, s))), ACT.Copy), ("VN", p, s))

            split_to(split_no[("gdnout", 0)] + 2)
            wait_evacuated(act, ("O", HEAD_PAIRS - 1, CHUNKS - 1))
            for h in range(GH + 1):
                if h < GH:
                    if h >= 2:
                        act.wait_ge(read32, h - 1)
                    nc.scalar.activation(gdn_sq[:, h % 2, 0:LAT], o_fm[:, h, :], ACT.Square).then_inc(read_sq, 1)
                if h:
                    rstd(gdn_sq[:, (h - 1) % 2, 0:LAT], bank(("osum", h - 1))[:, 0:LAT], ("osum", h - 1), 1.0 / P)

        def gdn_vector(dve, link):
            for n in range(len(GDN_STEPS) + 1):
                u = conv_step(n - CONV_LAG)
                if u is not None and CONV_TILES[u][0] == "v":
                    h = CONV_TILES[u][1]
                    wait_product(dve, ("vt", h))
                    release(nc.vector.tensor_copy(v_tok[:, :, h, :], units(bank(("vt", h)))), ("vt", h))
                u = conv_step(n)
                if n == 0:
                    key = ("gdn", "ab", 0)
                    wait_product(dve, key)
                    rows = lambda ap: ap.unsqueeze(1).to_broadcast([P, CHUNKS, 2 * GH])
                    link(nc.vector.tensor_tensor(gates[:, 0], bank(key)[:, 0:16 * GH].rearrange(
                        "p (c n) -> p c n", c=CHUNKS)[:, :, 0:2 * GH], rows(dt_row), ALU.add))
                    nc.vector.tensor_scalar(gates[:, 1], gates[:, 0], 0.0, None, ALU.max)
                    link(nc.vector.tensor_scalar(gates[:, 2], gates[:, 0], -1.0, None, ALU.mult))
                    nc.vector.tensor_tensor(gates[:, 2], gates[:, 2], gates[:, 0], ALU.min).then_inc(gate_pre, 1)
                if n == 1:
                    dve.wait_ge(gate_exp, 1)
                    link(nc.vector.tensor_tensor(gates[:, 1], gates[:, 1], gates[:, 2], ALU.add))
                    nc.vector.scalar_tensor_tensor(out=log_decay, in0=gates[:, 1], scalar=-1.0,
                                                   in1=alog_row.unsqueeze(1).to_broadcast([P, CHUNKS, 2 * GH]),
                                                   op0=ALU.mult, op1=ALU.mult).then_inc(gate_sp, 1)
                if n == 5:
                    wait_product(dve, ("cum", 0))
                    release(nc.vector.tensor_copy(cum_g, bank(("cum", 0))[:, 0:CHUNKS * 2 * GH].rearrange(
                        "p (c n) -> p c n", c=CHUNKS)), ("cum", 0))
                if n == 8:
                    dve.wait_ge(gate_decay, 1)
                    nc.vector.tensor_scalar(neg_decay, neg_decay, -1.0, None, ALU.mult).then_inc(gate_ready, 1)
                if u is not None:
                    kind, h = CONV_TILES[u]
                    wait_evacuated(dve, ("gdn", kind, h))
                    if u >= 2:
                        dve.wait_ge(conv_silu, u - 1)
                        if CONV_TILES[u - 2][0] == "v":
                            wait_product(dve, ("vt", CONV_TILES[u - 2][1]))
                    lo = conv_lo(u)
                    dst = conv_out[u % 2][:, lo:T].rearrange("p (s n) -> p s n", n=CTX)
                    src = conv_in[u % 2][:, lo // CTX:2, :]
                    tap = lambda j: conv_cols[:, (j * 3 * GH + CONV_CHANNEL[kind] + h):][:, 0:1]
                    link(nc.vector.tensor_scalar(dst, src[:, :, 0:CTX], tap(0), None, ALU.mult))
                    for j in range(1, 4):
                        ins = nc.vector.scalar_tensor_tensor(out=dst, in0=src[:, :, j:j + CTX], scalar=tap(j), in1=dst,
                                                             op0=ALU.mult, op1=ALU.add)
                        if j < 3:
                            link(ins)
                    ins.then_inc(conv_done, 1)

            for e in range(2 * GH):
                tile, width = norm_tile(e)
                wait_evacuated(dve, ("ksum", e))
                nc.vector.scalar_tensor_tensor(out=tile, in0=tile, scalar=1.0 if e < GH else GDN_SCALE,
                                               in1=gdn_sq[:, e % 2, 0:width], op0=ALU.mult,
                                               op1=ALU.mult).then_inc(normed, 1)
            dve.wait_ge(gate_ready, 1)
            dve.wait_ge(levels_ready, 1)

            for p in range(HEAD_PAIRS):
                for c in range(CHUNKS):
                    rows = units(bank(("R", p, c)))
                    wait_product(dve, ("R", p, c))
                    for unit in range(4):
                        last = nc.vector.tensor_scalar(z_mat[c][:, unit, :], rows[:, unit, :],
                                                       gate_cols(cum_g, c, unit, p), None, ALU.subtract)
                    link(last)
                    nc.vector.tensor_scalar(t_mat[c], z_mat[c], 0.0, None, ALU.max)
                    nc.vector.tensor_scalar(u_mat[c], z_mat[c], 0.0, None, ALU.min).then_inc(diffs_ready, 1)
                for c in range(CHUNKS):
                    g = units(bank(("G", p, c)))
                    wait_evacuated(dve, ("R", p, c))
                    wait_product(dve, ("G", p, c))
                    for d in range(2):
                        nc.vector.tensor_copy(wl[:, c, 2 * d:2 * d + 2], u_mat[c][:, 2 * d:2 * d + 2, end_col(d)])
                    if c >= LAT_CHUNK:
                        for d in range(2):
                            last = nc.vector.tensor_tensor(attnT[:, c - LAT_CHUNK, 2 * d:2 * d + 2, :], g[:, 2:4, :],
                                                           u_mat[c][:, 2 * d:2 * d + 2, :], ALU.mult)
                        last.then_inc(attn_raw, 1)
                    for unit in range(4):
                        last = nc.vector.scalar_tensor_tensor(
                            out=n_mat[c][:, unit, :], in0=g[:, unit % 2, :], scalar=gate_cols(beta_g, c, unit, p),
                            in1=t_mat[c][:, unit, :], op0=ALU.mult, op1=ALU.mult)
                    release(last, ("G", p, c))
                for level in range(LEVELS):
                    for c in range(CHUNKS):
                        buf = c % 2
                        by_dir = lambda ap: ap.rearrange("p (d h) n -> p d h n", d=2)
                        if 0 < level < LEVELS - 1:
                            dve.wait_ge(t_ready, p * (LEVELS - 1) * CHUNKS + level * CHUNKS + c - 1)
                            job = ("V", p, level, c)
                            wait_product(dve, job)
                            release(nc.vector.tensor_tensor(by_dir(masked_v[:, buf]), by_dir(units(bank(job))),
                                                            both(level_mask[:, level, 0:2, :]), ALU.mult), job)
                        job = ("NT", p, c) if level == 0 else ("W", p, level, c)
                        wait_product(dve, job)
                        release(nc.vector.tensor_tensor(by_dir(masked_w[:, buf]), by_dir(units(bank(job))),
                                                        both(level_mask[:, level, 1:3, :]), ALU.mult), job)
                        wait_evacuated(dve, job)
                        old = ident.unsqueeze(1).to_broadcast([P, 4, P]) if level == 0 else u_mat[c]
                        nc.vector.tensor_tensor(u_mat[c], old, masked_w[:, buf], ALU.subtract).then_inc(u_ready, 1)
                for s in range(CHUNKS):
                    cc = [scan_chunk(unit // 2, s) for unit in range(4)]
                    if s:
                        job = ("KS", p, s)
                        wait_product(dve, job)
                        for unit in range(4):
                            last = nc.vector.scalar_tensor_tensor(
                                out=scan_rhs[:, unit, :], in0=bank(job)[:, unit * P:(unit + 1) * P],
                                scalar=gate_cols(neg_decay, cc[unit], unit, p),
                                in1=v_tok[:, cc[unit], 2 * p + unit % 2, :], op0=ALU.mult, op1=ALU.add)
                        release(last, job)
                    if s < CHUNKS - 1:
                        wait_evacuated(dve, ("VN", p, s))
                        if s:
                            wait_product(dve, ("S", p, s - 1))
                        for unit in range(4):
                            last = nc.vector.tensor_scalar(v_end[:, unit, :], v_new[:, unit, :],
                                                           wl[:, cc[unit], unit:unit + 1], None, ALU.mult)
                        last.then_inc(v_end_ready, 1)
                        job = ("S", p, s)
                        wait_product(dve, job)
                        if s >= LAT_CHUNK:
                            wait_product(dve, ("O", p, s))
                        if s == 0:
                            release(nc.vector.tensor_copy(state, units(bank(job))), job)
                        else:
                            for unit in range(4):
                                last = nc.vector.scalar_tensor_tensor(
                                    out=state[:, unit, :], in0=state[:, unit, :],
                                    scalar=el[:, cc[unit], unit:unit + 1],
                                    in1=bank(job)[:, unit * P:(unit + 1) * P], op0=ALU.mult, op1=ALU.add)
                            release(last, job)
                    if s >= LAT_CHUNK:
                        job = ("O", p, s)
                        wait_product(dve, job)
                        for d in range(2):
                            at_ = (cc[2 * d] - LAT_CHUNK) * CHUNK
                            dst = o_fm[:, 2 * p:2 * p + 2, at_:at_ + CHUNK]
                            src = units(bank(job))[:, 2 * d:2 * d + 2, :]
                            if s == LAT_CHUNK:
                                last = nc.vector.tensor_copy(dst, src)
                            else:
                                last = nc.vector.tensor_tensor(dst, dst, src, ALU.add)
                        release(last, job)
                        if s == LAT_CHUNK:
                            wait_evacuated(dve, job)

            for h in range(GH):
                wait_evacuated(dve, ("osum", h))
                if h >= 2:
                    dve.wait_ge(o_lo_ready, KT + h - 1)
                link(nc.vector.scalar_tensor_tensor(out=read_t[:, h % 2, :], in0=o_fm[:, h, :],
                                                    scalar=colsA[:, R_GDN:R_GDN + 1], in1=gdn_sq[:, h % 2, 0:LAT],
                                                    op0=ALU.mult, op1=ALU.mult))
                nc.vector.tensor_tensor(read_t[:, h % 2, :], read_t[:, h % 2, :], z_fm[:, h, :],
                                        ALU.mult).then_inc(read32, 1)
                dve.wait_ge(read32, h + 1)
                nc.vector.tensor_copy(h_hi[:, h, CTX:T], read_t[:, h % 2, :]).then_inc(o_hi_ready, 1)

        def gdn_gpsimd(pool, link, split_to, split_o):
            pool.wait_ge(x_updated, 2 * KT)
            for n in range(2):
                nc.gpsimd.memset(conv_in[n][:, :, 0:2], 0.0)
                last = nc.gpsimd.memset(conv_in[n][:, :, CTX + 2:CTX + 3], 0.0)
            last.then_inc(pads_ready, 1)
            for n in range(len(GDN_STEPS)):
                split_to(split_no[("gdn",) + GDN_STEPS[n]] + 2)
            pool.wait_ge(normed, 2 * GH)
            for p in range(HEAD_PAIRS):
                for c in range(CHUNKS):
                    if p:
                        wait_evacuated(pool, ("O", p - 1, CHUNKS - 1))
                    elif c == 0:
                        wait_product(pool, ("gdn", "z", GH - 1))
                    for unit in range(4):
                        last = nc.gpsimd.tensor_scalar(n_mat[c][:, unit, :], tri[unit // 2],
                                                       gate_cols(log_decay, c, unit, p), one, ALU.mult, ALU.mult)
                    last.then_inc(tri_gates, 1)
                for c in range(LAT_CHUNK, CHUNKS):
                    lat = slice((c - LAT_CHUNK) * CHUNK, (c - LAT_CHUNK + 1) * CHUNK)
                    wait_evacuated(pool, ("R", p, c))
                    for d in range(2):
                        last = nc.gpsimd.tensor_tensor(q_dec[:, c - LAT_CHUNK, 2 * d:2 * d + 2, :],
                                                       q_fm[:, 2 * p:2 * p + 2, lat],
                                                       row_decay[:, c - LAT_CHUNK, 2 * d:2 * d + 2, :], ALU.mult)
                    pool.wait_ge(attn_raw, p * (CHUNKS - LAT_CHUNK) + c - LAT_CHUNK + 1)
                    for d in range(2):
                        part = attnT[:, c - LAT_CHUNK, 2 * d:2 * d + 2, :]
                        last = nc.gpsimd.tensor_tensor(part, part, tri[d].unsqueeze(1).to_broadcast([P, 2, P]),
                                                       ALU.mult)
                    last.then_inc(attn_ready, 1)
                for c in range(CHUNKS):
                    wait_evacuated(pool, ("G", p, c))
                    link(nc.gpsimd.tensor_tensor(t_mat[c].rearrange("p (d h) n -> p d h n", d=2),
                                                 n_mat[c].rearrange("p (d h) n -> p d h n", d=2),
                                                 both(level_mask[:, 0, 0:2, :]), ALU.mult))
                    nc.gpsimd.tensor_tensor(t_mat[c], ident.unsqueeze(1).to_broadcast([P, 4, P]), t_mat[c],
                                            ALU.subtract).then_inc(t_ready, 1)
                for level in range(1, LEVELS - 1):
                    for c in range(CHUNKS):
                        wait_evacuated(pool, ("V", p, level, c))
                        wait_product(pool, ("W", p, level, c))
                        nc.gpsimd.tensor_tensor(t_mat[c], t_mat[c], masked_v[:, c % 2],
                                                ALU.subtract).then_inc(t_ready, 1)
            for h in range(GH):
                pool.wait_ge(o_hi_ready, KT + h + 1)
                split_o(h, read_t[:, h % 2, :], CTX)

        block = stack.enter_context(nc.Block())

        @block.tensor
        def _(pe):
            jobs = [0]

            def finish(ins, job):
                jobs[0] += 1
                done_at[job] = jobs[0]
                ins.then_inc(products_done, 1)

            def take(job, ring="work"):
                b = RINGS[ring][taken[ring] % len(RINGS[ring])]
                taken[ring] += 1
                if used[b]:
                    pe.wait_ge(evacuated[b], used[b])
                used[b] += 1
                turn_of[job] = (b, used[b])
                return banks[b]

            def ada(ids):
                for n in ids:
                    if n == 0:
                        pe.wait_ge(silu_ready, 1)
                    if n % KT == 0 and n:
                        pe.wait_ge(ada_taken, n // KT)
                    wait_raw(pe, ("ada", n))
                    w = raw_slot(("ada", n))
                    for k in range(KT):
                        m = nc.tensor.matmul(banks[0][:, 2 * (n % KT):2 * (n % KT) + 2], w[:, k, :],
                                             silu_c[:, k, :], start=(k == 0), stop=(k == KT - 1))
                    finish(m, ("ada", n))

            def three(dst, stationary, moving, kk, first, last, before=None):
                for k in kk:
                    if before:
                        before(k)
                    for a, b in ((0, 0), (0, 1), (1, 0)):
                        m = nc.tensor.matmul(dst, stationary(a, k), moving(b, k),
                                             start=(first and k == kk[0] and a == b == 0),
                                             stop=(last and k == kk[-1] and a == 1))
                return m

            def weights(key):
                n = split_no[key]
                pe.wait_ge(w_hi_ready, n + 1)
                pe.wait_ge(w_lo_ready, n + 1)
                slot = (w_hi[n % N_SPLIT], w_lo[n % N_SPLIT])
                return lambda part, k: slot[part][:, k, :]

            def h_waits(i):
                return None if i is None else (lambda k: pe.wait_ge(h_ready, i * KT + k + 1))

            def project(key, job, lo, first_of=None):
                dst = take(job)[:, lo:T]
                m = three(dst, weights(key), lambda part, k: (h_hi, h_lo)[part][:, k, lo:T],
                          range(KT), True, True, before=h_waits(first_of))
                finish(m, job)

            def project_tokens(key, job, width, first_of=None):
                dst = take(job)
                w = weights(key)
                for t in range(T // P):
                    m = three(dst[:, t * width:(t + 1) * width],
                              lambda part, k: (h_hi, h_lo)[part][:, k, t * P:(t + 1) * P],
                              lambda part, k: w(part, k)[:, 0:width], range(KT), True, True,
                              before=h_waits(first_of) if t == 0 else None)
                finish(m, job)

            def pre_norm(i):
                lo = first_token(i)
                dst = take(("pre", i), "side")
                for k in range(KT):
                    pe.wait_ge(pre_sq_ready, i * KT + k + 1)
                    m = nc.tensor.matmul(dst[:, lo:T], ones, pre_sq[:, k % 2, lo:T],
                                         start=(k == 0), stop=(k == KT - 1))
                    finish(m, ("pre_sq", i, k))
                done_at[("pre", i)] = jobs[0]

            def post_norm(i):
                lo = first_out(i)
                pe.wait_ge(y_acc_ready, (i + 1) * KT)
                dst = take(("post", i), "side")
                finish(nc.tensor.matmul(dst[:, lo:T], ones, post_views[i][3][:, lo:T],
                                        start=True, stop=True), ("post", i))

            def out_project(i, name, base):
                for m in range(KT):
                    if m == 0:
                        pe.wait_ge(o_hi_ready, base)
                        pe.wait_ge(o_lo_ready, base)
                    project((name, m), ("y", i, m), first_out(i))

            def ffn(layer):
                i = 2 * layer + 1
                lo = first_token(i)
                for n in range(2 * FT):
                    project(("gate", layer, n), ("gate", layer, n), lo, i if n == 0 else None)
                    ada(ada_after(f"gate{layer}", n))
                for m in range(KT):
                    dst = take(("y", i, m))[:, lo:T]
                    for part, (a, b) in enumerate(DOWN_PARTS):
                        w = weights(("down", layer, m, part))

                        def hidden_there(k):
                            pe.wait_ge(act_hi_ready, layer * FT + k + 1)
                            pe.wait_ge(act_lo_ready, layer * FT + k + 1)
                        last = three(dst, lambda p, k: w(p, k - a),
                                     lambda p, k: (act_hi, act_lo)[p][:, k, lo:T], range(a, b),
                                     part == 0, part == 2, before=hidden_there if m == 0 else None)
                        finish(last, ("down", layer, m, part))
                    done_at[("y", i, m)] = jobs[0]
                    ada(ada_after(f"down{layer}", m))

            pe.wait_ge(tables_in, 16)
            pe.wait_ge(rows_in, 16 * ROW_DMAS)
            for n, (rows, count) in enumerate(((rowsA, R_N), (rowsB, 2 * 6 * KT), (rowsC, 4 * 3 * GH))):
                dst = take(("cols", n))
                finish(nc.tensor.transpose(dst[:, 0:count], rows[0:count, :], ident[0:count, 0:count]),
                       ("cols", n))
            pe.wait_ge(tok_in, 16 * 2)
            for k in range(KT):
                dst = take(("x", k))
                for t in range(4):
                    m = nc.tensor.transpose(dst[:, t * P:(t + 1) * P], tok[:, t, k * P:(k + 1) * P], ident)
                finish(m, ("x", k))
            pre_norm(0)
            ada(ada_after("start", 0))

            for n in range(len(QKV_STEPS) + 2):
                if n < len(QKV_STEPS):
                    key = ("qkv",) + QKV_STEPS[n]
                    if QKV_STEPS[n][0] in ("gv", "dv"):
                        project_tokens(key, key, P, 0 if n == 0 else None)
                    else:
                        project(key, key, 0, 0 if n == 0 else None)
                    ada(ada_after("qkv", n))
                for u in stat_at(n):
                    wait_evacuated(pe, ("qkv",) + QK_TILES[u])
                    finish(nc.tensor.matmul(take(("qk_stat", u), "side"), block_ones, qk_sq[:, u % 2, :],
                                            start=True, stop=True), ("qk_stat", u))
                for u in rotate_at(n):
                    if u in NORMED:
                        pe.wait_ge(qk_normed, NORMED.index(u) + 1)
                    else:
                        wait_evacuated(pe, ("qkv",) + QK_TILES[u])
                    dst = take(("rot", u))
                    finish(nc.tensor.matmul(dst[:, 0:LAT], rotation, qk_n[:, u % 3, CTX:T],
                                            start=True, stop=True), ("rot", u))

            def scores(n):
                head, qb = ATT_UNITS[n]
                for m, (qt, half, kt) in enumerate(maps_of(head)):
                    if qb == 0:
                        pe.wait_ge(qk_out, 5 + qt + 1)
                    dst = take(("s", n, m))
                    finish(nc.tensor.matmul(dst[:, 0:keys_of(qb)], q_sb[:, qt, half, qb * P:(qb + 1) * P],
                                            k_sb[:, kt, 0:keys_of(qb)], start=True, stop=True), ("s", n, m))

            def turn(n):
                qb = ATT_UNITS[n][1]
                pe.wait_ge(probs_ready, n + 1)
                dst = take(("t", n))
                for t in range(keys_of(qb) // P):
                    m = nc.tensor.transpose(dst[:, t * P:(t + 1) * P],
                                            probs[:, n % 3, 0, t * P:(t + 1) * P], ident)
                finish(m, ("t", n))

            def values(n):
                head, qb = ATT_UNITS[n]
                if n == 0:
                    wait_evacuated(pe, ("qkv", "dv", 3))
                if qb == 0:
                    take(("o", head), "side")
                dst = bank(("o", head))
                wait_evacuated(pe, ("t", n))
                c0 = head * P if head < DIFF_HEADS else 512 + (head - DIFF_HEADS) // 4 * P
                tiles = keys_of(qb) // P
                for t in range(tiles):
                    m = nc.tensor.matmul(dst[:, qb * P:(qb + 1) * P], v_sb[:, t, c0:c0 + P],
                                         probsT[:, n % 2, t, :], start=(t == 0), stop=(t == tiles - 1))
                finish(m, ("v", n))
                done_at[("o", head)] = jobs[0]

            for n in range(len(ATT_UNITS) + 4):
                if n < len(ATT_UNITS):
                    scores(n)
                    ada(ada_after("att", n))
                if 3 <= n < len(ATT_UNITS) + 3:
                    values(n - 3)
                if 2 <= n < len(ATT_UNITS) + 2:
                    turn(n - 2)
                if n in SUBLN_AT:
                    h = SUBLN_AT.index(n)
                    wait_evacuated(pe, ("o", h))
                    finish(nc.tensor.matmul(take(("o_stat", h)), ones, o_sq, start=True, stop=True),
                           ("o_stat", h))
            out_project(0, "attout", KT)
            post_norm(0)
            pre_norm(1)
            ffn(0)
            post_norm(1)
            if LAST_SUB == 3:
                pre_norm(2)
                gdn_tensor(pe, take, finish, project, project_tokens)
                out_project(2, "gdnout", 2 * KT)
                post_norm(2)
                pre_norm(3)
                ffn(1)
                post_norm(3)
            pe.wait_ge(x_updated, (LAST_SUB + 1) * KT)
            for t in range(LAT // P):
                for half in range(2):
                    dst = take(("out", t, half))
                    for k in range(4):
                        m = nc.tensor.transpose(dst[:, k * P:(k + 1) * P],
                                                xT[:, 4 * half + k, CTX + t * P:CTX + (t + 1) * P], ident)
                    finish(m, ("out", t, half))

        @block.scalar
        def _(act):
            chain = [0]
            splits = [0]

            def link(ins):
                chain[0] += 1
                ins.then_inc(act_chain, 1)
                act.wait_ge(act_chain, chain[0])

            def split_to(n):
                while splits[0] <= min(n, len(split_keys) - 1):
                    m = splits[0]
                    key = split_keys[m]
                    if m >= N_SPLIT:
                        wait_product(act, split_job(split_keys[m - N_SPLIT]))
                    wait_raw(act, key)
                    w = chunk_width(key)
                    nc.scalar.activation(w_hi[m % N_SPLIT][:, :, 0:w], raw_slot(key)[:, :, 0:w],
                                         ACT.Copy).then_inc(w_hi_ready, 1)
                    splits[0] += 1

            def rstd(dst, src, job, scale):
                wait_product(act, job)
                link(nc.scalar.activation(dst, src, ACT.Ln, bias=eps, scale=scale))
                release(nc.scalar.activation(dst, dst, ACT.Exp, scale=-0.5), job)

            def pre_norm(i):
                lo = first_token(i)
                layer, part = i // 2, 3 * (i % 2)
                if i:
                    split_to(split_no[FIRST_CHUNK[i]] + 2)
                for k in range(KT):
                    x_ready(act, i, k)
                    if k >= 2:
                        wait_product(act, ("pre_sq", i, k - 2))
                    nc.scalar.activation(pre_sq[:, k % 2, lo:T], xT[:, k, lo:T],
                                         ACT.Square).then_inc(pre_sq_ready, 1)
                rstd(pre_rstd[:, lo:T], bank(("pre", i))[:, lo:T], ("pre", i), 1.0 / D)
                split_to(split_no[FIRST_CHUNK[i]] + 2)
                act.wait_ge(mods_ready, layer * 4 + (3 if part else 1))
                for k in range(KT):
                    act.wait_ge(pre_t_ready, i * KT + k + 1)
                    if k >= 2:
                        act.wait_ge(h_ready, i * KT + k - 1)
                    for s in range(lo // CTX, 2):
                        a, b = STREAMS[s]
                        last = nc.scalar.activation(pre_h[:, k % 2, a:b], pre_t[:, k % 2, a:b],
                                                    ACT.Identity, scale=mod_col(layer, part + 1, k, s),
                                                    bias=mod_col(layer, part, k, s))
                    last.then_inc(h32_ready, 1)

            def take_y(i, m):
                lo = first_out(i)
                wait_product(act, ("y", i, m))
                if m >= 2:
                    act.wait_ge(y_acc_ready, i * KT + m - 1)
                nc.scalar.activation(post_views[i][2][:, m % 2, lo:T], bank(("y", i, m))[:, lo:T], ACT.Square)
                release(nc.scalar.activation(y_views[i][:, m, lo:T], bank(("y", i, m))[:, lo:T], ACT.Copy),
                        ("y", i, m))

            def post_norm(i):
                lo = first_out(i)
                rstd(post_views[i][0][:, lo:T], bank(("post", i))[:, lo:T], ("post", i), 1.0 / D)

            def out_project(i, name):
                for m in range(KT):
                    split_to(split_no[(name, m)] + 2)
                    take_y(i, m)

            def ffn(layer):
                i = 2 * layer + 1
                lo = first_token(i)
                for n in range(2 * FT):
                    key = ("gate", layer, n)
                    j = layer * FT + n // 2
                    split_to(split_no[key] + 2)
                    if n % 2 == 0:
                        wait_product(act, key)
                        if n >= 4:
                            wait_evacuated(act, ("gate", layer, n - 3))
                        release(nc.scalar.activation(s_tmp[:, j % 2, lo:T], bank(key)[:, lo:T], ACT.Silu), key)
                    else:
                        wait_evacuated(act, key)
                        nc.scalar.activation(act_hi[:, n // 2, lo:T], a_tmp[:, j % 2, lo:T],
                                             ACT.Copy).then_inc(act_hi_ready, 1)
                for m in range(KT):
                    split_to(split_no[("down", layer, m, 2)] + 2)
                    take_y(i, m)

            wait_evacuated(act, ("cols", 0))
            nc.scalar.activation(silu_c, colsA[:, R_C:R_C + 2 * KT].rearrange("p (s k) -> p k s", s=2),
                                 ACT.Silu).then_inc(silu_ready, 1)
            act.wait_ge(lam_sums, 1)
            nc.scalar.activation(lam_two[:, 2:4], lam_two[:, 0:2], ACT.Exp).then_inc(lam_exps, 1)
            pre_norm(0)
            for n in range(len(QKV_STEPS) + 2):
                if n < len(QKV_STEPS):
                    key = ("qkv",) + QKV_STEPS[n]
                    split_to(min(split_no[key], split_no[("qkv", "gq", 3)] - 2) + 2)
                    if QKV_STEPS[n] in QK_TILES:
                        u = QK_TILES.index(QKV_STEPS[n])
                        wait_product(act, key)
                        if u >= 3:
                            act.wait_ge(qk_out, u - 2)
                        if u in NORMED:
                            if u - 2 in NORMED:
                                act.wait_ge(qk_normed, NORMED.index(u - 2) + 1)
                            nc.scalar.activation(qk_sq[:, u % 2, :], bank(key), ACT.Square)
                        release(nc.scalar.activation(qk_n[:, u % 3, :], bank(key), ACT.Copy), key)
                for u in stat_at(n):
                    rstd(qk_sq[:, u % 2, :], bank(("qk_stat", u)), ("qk_stat", u), 1.0 / HEAD)

            for n in range(len(ATT_UNITS) + 4):
                if n < len(ATT_UNITS):
                    head, qb = ATT_UNITS[n]
                    for m in range(len(maps_of(head))):
                        act.wait_ge(max_ready, map_no(n, m) + 1)
                        if n >= 3:
                            wait_product(act, ("t", n - 3))
                        release(nc.scalar.activation(probs[:, n % 3, m, 0:keys_of(qb)],
                                                     bank(("s", n, m))[:, 0:keys_of(qb)], ACT.Exp,
                                                     bias=stats[:, n % 4, m:m + 1],
                                                     accum_out=stats[:, n % 4, 2 + m:3 + m]), ("s", n, m))
                if 3 <= n < len(ATT_UNITS) + 3 and ATT_UNITS[n - 3][1] == 3:
                    head = ATT_UNITS[n - 3][0]
                    src = bank(("o", head))
                    wait_product(act, ("o", head))
                    if head == 0:
                        act.wait_ge(qk_out, len(QK_TILES))
                    if head < DIFF_HEADS:
                        if head:
                            act.wait_ge(o_scaled, head)
                        nc.scalar.activation(o_sq, src, ACT.Square)
                        release(nc.scalar.activation(o_sb[:, head, :], src, ACT.Copy), ("o", head))
                    else:
                        tile, half = divmod(head - DIFF_HEADS, 2)
                        rows = slice(half * HEAD, (half + 1) * HEAD)
                        release(nc.scalar.activation(o_sb[rows, DIFF_HEADS + tile, :], src[rows, :], ACT.Copy),
                                ("o", head))
                if 2 <= n < len(ATT_UNITS) + 2:
                    keys = keys_of(ATT_UNITS[n - 2][1])
                    wait_product(act, ("t", n - 2))
                    if n >= 4:
                        wait_product(act, ("v", n - 4))
                    release(nc.scalar.activation(probsT[:, (n - 2) % 2, 0:keys // P, :],
                                                 units(bank(("t", n - 2))[:, 0:keys]), ACT.Copy), ("t", n - 2))
                if n == 44:
                    split_to(split_no[("attout", 0)] + 2)
                if n in SUBLN_AT:
                    h = SUBLN_AT.index(n)
                    rstd(o_sq, bank(("o_stat", h)), ("o_stat", h), 1.0 / P)
            out_project(0, "attout")
            post_norm(0)
            pre_norm(1)
            ffn(0)
            post_norm(1)
            if LAST_SUB == 3:
                pre_norm(2)
                gdn_scalar(act, link, split_to, rstd)
                out_project(2, "gdnout")
                post_norm(2)
                pre_norm(3)
                ffn(1)
                post_norm(3)

        @block.vector
        def _(dve):
            chain = [0]

            def link(ins):
                chain[0] += 1
                ins.then_inc(dve_chain, 1)
                dve.wait_ge(dve_chain, chain[0])

            def ada(ids):
                for n in ids:
                    if n % KT < KT - 1:
                        continue
                    layer, part = divmod(n // KT, 6)
                    wait_product(dve, ("ada", n))
                    dst = mods[:, layer, part, :, :]
                    col = (layer * 6 + part) * KT
                    nc.vector.tensor_tensor(dst, banks[0][:, 0:2 * KT].rearrange("p (k s) -> p k s", s=2),
                                            ada_bias[:, col:col + KT].unsqueeze(2).to_broadcast([P, KT, 2]),
                                            ALU.add).then_inc(ada_taken, 1)
                    if part % 3:
                        dve.wait_ge(ada_taken, n // KT + 1)
                        g = R_NORM + (layer * 4 + (part // 3) * 2 + part % 3 - 1) * KT
                        gain = colsA[:, g:g + KT].unsqueeze(2).to_broadcast([P, KT, 2])
                        nc.vector.scalar_tensor_tensor(out=dst, in0=dst, scalar=float(part % 3 == 1), in1=gain,
                                                       op0=ALU.add, op1=ALU.mult).then_inc(mods_ready, 1)

            def pre_norm(i):
                lo = first_token(i)
                for k in range(KT):
                    dve.wait_ge(h32_ready, i * KT + k + 1)
                    link(nc.vector.tensor_copy(h_hi[:, k, lo:T], pre_h[:, k % 2, lo:T]))
                    nc.vector.tensor_tensor(h_lo[:, k, lo:T], pre_h[:, k % 2, lo:T],
                                            h_hi[:, k, lo:T].bitcast(F32), ALU.subtract).then_inc(h_ready, 1)

            def sum_y(i, m):
                lo = first_out(i)
                acc, sq = post_views[i][3][:, lo:T], post_views[i][2][:, m % 2, lo:T]
                wait_evacuated(dve, ("y", i, m))
                if m == 0:
                    nc.vector.tensor_copy(acc, sq).then_inc(y_acc_ready, 1)
                else:
                    dve.wait_ge(y_acc_ready, i * KT + m)
                    nc.vector.tensor_tensor(acc, acc, sq, ALU.add).then_inc(y_acc_ready, 1)

            def post_norm(i):
                layer, part = i // 2, 3 * (i % 2) + 2
                dve.wait_ge(mods_ready, layer * 4 + (4 if i % 2 else 2))
                for k in range(KT):
                    dve.wait_ge(post_t_ready, i * KT + k + 1)
                    for s in range(first_out(i) // CTX, 2):
                        a, b = STREAMS[s]
                        last = nc.vector.scalar_tensor_tensor(
                            out=xT[:, k, a:b], in0=post_views[i][1][:, k % 2, a:b],
                            scalar=mod_col(layer, part, k, s), in1=xT[:, k, a:b], op0=ALU.mult, op1=ALU.add)
                    last.then_inc(x_updated, 1)

            def ffn(layer):
                i = 2 * layer + 1
                lo = first_token(i)
                for n in range(2 * FT):
                    if n % 2:
                        j = layer * FT + n // 2
                        key = ("gate", layer, n)
                        wait_product(dve, key)
                        wait_evacuated(dve, ("gate", layer, n - 1))
                        if n >= 5:
                            dve.wait_ge(act_lo_ready, j - 1)
                        release(nc.vector.tensor_tensor(a_tmp[:, j % 2, lo:T], bank(key)[:, lo:T],
                                                        s_tmp[:, j % 2, lo:T], ALU.mult), key)
                    ada(ada_after(f"gate{layer}", n))
                for m in range(KT):
                    sum_y(i, m)
                    ada(ada_after(f"down{layer}", m))

            for n, (cols, count) in enumerate(((colsA, R_N), (ada_bias, 2 * 6 * KT), (conv_cols, 4 * 3 * GH))):
                wait_product(dve, ("cols", n))
                release(nc.vector.tensor_copy(cols[:, 0:count], bank(("cols", n))[:, 0:count]), ("cols", n))
            lam_pairs = lam_row.rearrange("p (a b d) -> p a b d", a=2, b=2)
            link(nc.vector.tensor_tensor(lam_pairs[:, :, 0, :], lam_pairs[:, :, 0, :], lam_pairs[:, :, 1, :],
                                         ALU.mult))
            nc.vector.tensor_reduce(lam_two[:, 0:2], lam_pairs[:, :, 0, :], AXIS_X, ALU.add).then_inc(lam_sums, 1)
            for k in range(KT):
                wait_product(dve, ("x", k))
                release(nc.vector.tensor_copy(xT[:, k, :], bank(("x", k))), ("x", k))
            dve.wait_ge(levels_in, 16)
            nc.vector.tensor_copy(level_mask.rearrange("p a b c -> p (a b c)"), level_f32).then_inc(levels_ready, 1)
            dve.wait_ge(lam_exps, 1)
            link(nc.vector.tensor_tensor(lam_two[:, 4:5], lam_two[:, 3:4], lam_two[:, 2:3], ALU.subtract))
            nc.vector.tensor_scalar(lam_two[:, 4:5], lam_two[:, 4:5], -LAM_INIT, None, ALU.add)
            nc.vector.tensor_scalar(sub_gain, colsA[:, R_SUB:R_SUB + 1], 1.0 - LAM_INIT, None,
                                    ALU.mult).then_inc(lam_ready, 1)
            ada(ada_after("start", 0))
            pre_norm(0)

            for n in range(len(QKV_STEPS) + 2):
                if n < len(QKV_STEPS):
                    kind, t = QKV_STEPS[n]
                    key = ("qkv", kind, t)
                    if kind in ("gv", "dv"):
                        wait_product(dve, key)
                        src = units(bank(key))
                        if kind == "dv":
                            release(nc.vector.tensor_copy(v_sb[:, :, t * P:(t + 1) * P], src), key)
                        else:
                            dst = v_sb[:, :, 512:768].rearrange("p t (g r d) -> p t g r d", g=GQA_KV, r=2)
                            src = src.rearrange("p t (g d) -> p t g d", g=GQA_KV)
                            nc.vector.tensor_copy(dst[:, :, :, 0, :], src)
                            release(nc.vector.tensor_copy(dst[:, :, :, 1, :], src), key)
                    ada(ada_after("qkv", n))
                for u in stat_at(n):
                    wait_evacuated(dve, ("qk_stat", u))
                    gain = colsA[:, R_QKG + (0 if QK_TILES[u][0] == "gq" else 1):][:, 0:1]
                    nc.vector.scalar_tensor_tensor(out=qk_n[:, u % 3, :], in0=qk_n[:, u % 3, :], scalar=gain,
                                                   in1=qk_sq[:, u % 2, :], op0=ALU.mult,
                                                   op1=ALU.mult).then_inc(qk_normed, 1)
                for u in rotate_at(n):
                    wait_product(dve, ("rot", u))
                    if u >= 2:
                        dve.wait_ge(qk_roped, u - 1)
                    release(nc.vector.tensor_tensor(qk_sined[:, u % 2, :], bank(("rot", u))[:, 0:LAT], sinT,
                                                    ALU.mult), ("rot", u))
                    wait_evacuated(dve, ("rot", u))
                    dve.wait_ge(qk_cos, u + 1)
                    nc.vector.tensor_tensor(qk_n[:, u % 3, CTX:T], qk_cosed[:, u % 2, :], qk_sined[:, u % 2, :],
                                            ALU.add).then_inc(qk_roped, 1)

            def maxima(n):
                head, qb = ATT_UNITS[n]
                for m in range(len(maps_of(head))):
                    wait_product(dve, ("s", n, m))
                    nc.vector.tensor_reduce(stats[:, n % 4, m:m + 1], bank(("s", n, m))[:, 0:keys_of(qb)], AXIS_X,
                                            ALU.max, negate=True).then_inc(max_ready, 1)

            def normalize(n):
                head, qb = ATT_UNITS[n]
                maps = len(maps_of(head))
                p = probs[:, n % 3, :, 0:keys_of(qb)]
                for m in range(maps):
                    wait_evacuated(dve, ("s", n, m))
                link(nc.vector.reciprocal(stats[:, n % 4, 4:4 + maps], stats[:, n % 4, 2:2 + maps]))
                first = nc.vector.tensor_scalar(p[:, 0, :], p[:, 0, :], stats[:, n % 4, 4:5], None, ALU.mult)
                if maps == 1:
                    first.then_inc(probs_ready, 1)
                    return
                link(first)
                if n == 0:
                    dve.wait_ge(lam_ready, 1)
                link(nc.vector.tensor_tensor(stats[:, n % 4, 5:6], stats[:, n % 4, 5:6], lam_two[:, 4:5], ALU.mult))
                nc.vector.scalar_tensor_tensor(out=p[:, 0, :], in0=p[:, 1, :], scalar=stats[:, n % 4, 5:6],
                                               in1=p[:, 0, :], op0=ALU.mult, op1=ALU.add).then_inc(probs_ready, 1)

            def split_o(tile):
                nc.vector.tensor_copy(h_hi[:, tile, :], o_sb[:, tile, :]).then_inc(o_hi_ready, 1)

            for n in range(len(ATT_UNITS) + 4):
                if n < len(ATT_UNITS):
                    maxima(n)
                    ada(ada_after("att", n))
                if 1 <= n < len(ATT_UNITS) + 1:
                    normalize(n - 1)
                if 3 <= n < len(ATT_UNITS) + 3 and ATT_UNITS[n - 3][1] == 3:
                    head = ATT_UNITS[n - 3][0]
                    if head >= DIFF_HEADS and head % 2:
                        wait_evacuated(dve, ("o", head - 1))
                        wait_evacuated(dve, ("o", head))
                        split_o(DIFF_HEADS + (head - DIFF_HEADS) // 2)
                if n in SUBLN_AT:
                    h = SUBLN_AT.index(n)
                    wait_evacuated(dve, ("o_stat", h))
                    nc.vector.scalar_tensor_tensor(out=o_sb[:, h, :], in0=o_sb[:, h, :], scalar=sub_gain,
                                                   in1=o_sq, op0=ALU.mult, op1=ALU.mult).then_inc(o_scaled, 1)
                    dve.wait_ge(o_scaled, h + 1)
                    split_o(h)
            for m in range(KT):
                sum_y(0, m)
            post_norm(0)
            pre_norm(1)
            ffn(0)
            post_norm(1)
            if LAST_SUB == 3:
                pre_norm(2)
                gdn_vector(dve, link)
                for m in range(KT):
                    sum_y(2, m)
                post_norm(2)
                pre_norm(3)
                ffn(1)
                post_norm(3)
            for t in range(LAT // P):
                for half in range(2):
                    job = ("out", t, half)
                    wait_product(dve, job)
                    release(nc.vector.tensor_copy(out_sb[:, t, half * 512:(half + 1) * 512], bank(job)), job)

        @block.gpsimd
        def _(pool):
            chain = [0]
            splits = [0]

            def link(ins):
                chain[0] += 1
                ins.then_inc(pool_chain, 1)
                pool.wait_ge(pool_chain, chain[0])

            def split_to(n):
                while splits[0] <= min(n, len(split_keys) - 1):
                    m = splits[0]
                    key = split_keys[m]
                    w = chunk_width(key)
                    pool.wait_ge(w_hi_ready, m + 1)
                    nc.gpsimd.tensor_tensor(w_lo[m % N_SPLIT][:, :, 0:w], raw_slot(key)[:, :, 0:w],
                                            w_hi[m % N_SPLIT][:, :, 0:w].bitcast(F32),
                                            ALU.subtract).then_inc(w_lo_ready, 1)
                    splits[0] += 1

            def pre_norm(i):
                lo = first_token(i)
                if i:
                    split_to(split_no[FIRST_CHUNK[i]] + 2)
                wait_evacuated(pool, ("pre", i))
                for k in range(KT):
                    if k == 2:
                        split_to(split_no[FIRST_CHUNK[i]] + 2)
                    if k >= 2:
                        pool.wait_ge(h32_ready, i * KT + k - 1)
                    nc.gpsimd.tensor_tensor(pre_t[:, k % 2, lo:T], xT[:, k, lo:T], pre_rstd[:, lo:T],
                                            ALU.mult).then_inc(pre_t_ready, 1)

            def post_norm(i):
                lo = first_out(i)
                wait_evacuated(pool, ("post", i))
                for k in range(KT):
                    if k >= 2:
                        pool.wait_ge(x_updated, i * KT + k - 1)
                    nc.gpsimd.tensor_tensor(post_views[i][1][:, k % 2, lo:T], y_views[i][:, k, lo:T],
                                            post_views[i][0][:, lo:T], ALU.mult).then_inc(post_t_ready, 1)

            def ffn(layer):
                lo = first_token(2 * layer + 1)
                for n in range(2 * FT):
                    split_to(split_no[("gate", layer, n)] + 2)
                    if n % 2:
                        j = layer * FT + n // 2
                        pool.wait_ge(act_hi_ready, j + 1)
                        nc.gpsimd.tensor_tensor(act_lo[:, n // 2, lo:T], a_tmp[:, j % 2, lo:T],
                                                act_hi[:, n // 2, lo:T].bitcast(F32),
                                                ALU.subtract).then_inc(act_lo_ready, 1)
                for m in range(KT):
                    split_to(split_no[("down", layer, m, 2)] + 2)

            def split_o(tile, src, lo):
                nc.gpsimd.tensor_tensor(h_lo[:, tile, lo:T], src, h_hi[:, tile, lo:T].bitcast(F32),
                                        ALU.subtract).then_inc(o_lo_ready, 1)

            pre_norm(0)
            for n in range(len(QKV_STEPS) + 2):
                if n < len(QKV_STEPS):
                    split_to(min(split_no[("qkv",) + QKV_STEPS[n]], split_no[("qkv", "gq", 3)] - 2) + 2)
                for u in rotate_at(n):
                    if u in NORMED:
                        pool.wait_ge(qk_normed, NORMED.index(u) + 1)
                    else:
                        wait_evacuated(pool, ("qkv",) + QK_TILES[u])
                    if u >= 2:
                        pool.wait_ge(qk_roped, u - 1)
                    nc.gpsimd.tensor_tensor(qk_cosed[:, u % 2, :], qk_n[:, u % 3, CTX:T], cosT,
                                            ALU.mult).then_inc(qk_cos, 1)
                    pool.wait_ge(qk_roped, u + 1)
                    if u < 5:
                        last = nc.gpsimd.tensor_copy(k_sb[:, u, :], qk_n[:, u % 3, :])
                    else:
                        for half in range(2):
                            last = nc.gpsimd.tensor_scalar(q_sb[:, u - 5, half, :], qk_n[:, u % 3, :],
                                                           tab[:, C_HALF + half:C_HALF + half + 1], one,
                                                           ALU.mult, ALU.mult)
                    last.then_inc(qk_out, 1)
            for tile in range(KT):
                pool.wait_ge(o_hi_ready, tile + 1)
                if tile == KT - 1:
                    split_to(split_no[("attout", 0)] + 2)
                split_o(tile, o_sb[:, tile, :], 0)
            for m in range(KT):
                split_to(split_no[("attout", m)] + 2)
            post_norm(0)
            pre_norm(1)
            ffn(0)
            post_norm(1)
            if LAST_SUB == 3:
                pre_norm(2)
                gdn_gpsimd(pool, link, split_to, split_o)
                for m in range(KT):
                    split_to(split_no[("gdnout", m)] + 2)
                post_norm(2)
                pre_norm(3)
                ffn(1)
                post_norm(3)

        @block.sync
        def _(sp):
            def columns(w, lo, width=P):
                return w[:, lo:lo + width].rearrange("(k p) m -> p k m", p=P)

            def source(key):
                kind = key[0]
                if kind == "ada":
                    layer, col = divmod(key[1], 6 * KT)
                    return columns(ada_w[layer], col * P)
                if kind == "qkv":
                    col = {"gk": GK_COL, "gv": GV_COL, "dk": DK_COL, "dv": DV_COL, "dq": DQ_COL}
                    return columns(attn_w_in[0], col[key[1]] + key[2] * P)
                if kind == "attout":
                    return columns(attn_w_out[0], key[1] * P)
                if kind == "gate":
                    j, up = divmod(key[2], 2)
                    return columns(ffn_w_gate_up[key[1]], up * FFN + j * P)
                if kind == "down":
                    a, b = DOWN_PARTS[key[3]]
                    return columns(ffn_w_down[key[1]][a * P:b * P, :], key[2] * P)
                if kind == "gdn":
                    col = {"q": 0, "k": GW, "v": 2 * GW, "z": 3 * GW, "ab": 4 * GW}[key[1]]
                    return columns(gdn_w_in[0], col + key[2] * P, chunk_width(key))
                return columns(gdn_w_out[0], key[1] * P)

            vec = lambda a, n: a.rearrange("(r p) -> r p", p=P)
            sp.dma_start(tab, tables).then_inc(tables_in, 16)
            row_dmas = [
                (rowsA[R_NORM:R_NORM + 64, :], norm_g.rearrange("l n (k p) -> (l n k) p", p=P)),
                (rowsA[R_C:R_C + 8, :], c_ctx.rearrange("(k p) -> k p", p=P)),
                (rowsA[R_C + 8:R_C + 16, :], c.rearrange("b (k p) -> (b k) p", p=P)),
                (rowsA[R_SUB:R_SUB + 1, :], diff_subln_g),
                (rowsA[R_GDN:R_GDN + 1, :], gdn_norm_g),
                (rowsA[R_QKG:R_QKG + 2, 0:HEAD], gqa_qk_g[0]),
                (rowsA[R_QKG:R_QKG + 2, HEAD:P], gqa_qk_g[0]),
                (rowsB[0:2 * 6 * KT, :], ada_b.rearrange("l (k p) -> (l k) p", p=P)),
                (rowsC[0:4 * 3 * GH, :], gdn_conv_w[0].rearrange("j (k p) -> (j k) p", p=P)),
                (lam_row, diff_lambda[0].rearrange("a d -> (a d)").partition_broadcast(P)),
                (dt_row, gdn_dt_bias[0].rearrange("a d -> (a d)").partition_broadcast(P)),
                (alog_row, gdn_a_log[0].rearrange("a d -> (a d)").partition_broadcast(P)),
            ]
            assert len(row_dmas) == ROW_DMAS
            for dst, src in row_dmas:
                sp.dma_start(dst, src).then_inc(rows_in, 16)
            sp.dma_start(tok[:, 0:2, :], ctx[0].rearrange("(t p) d -> p t d", p=P)).then_inc(tok_in, 16)
            sp.dma_start(tok[:, 2:4, :], x[0].rearrange("(t p) d -> p t d", p=P)).then_inc(tok_in, 16)
            sp.dma_start(level_f32, levels).then_inc(levels_in, 16)
            for n, key in enumerate(chunks):
                if n >= N_RAW:
                    last = chunks[n - N_RAW]
                    if last[0] == "ada":
                        wait_product(sp, last)
                    else:
                        sp.wait_ge(w_lo_ready, split_no[last] + 1)
                slot, done = w_raw[n % N_RAW], raw_in[n % N_RAW]
                if key[:2] == ("qkv", "gq"):
                    for g in range(GQA_KV):
                        col = GQ_COL + g * (GQA_HEADS // GQA_KV) * HEAD + key[2] * HEAD
                        sp.dma_start(slot[:, :, g * HEAD:(g + 1) * HEAD],
                                     columns(attn_w_in[0], col, HEAD)).then_inc(done, 16)
                else:
                    src = source(key)
                    sp.dma_start(slot[:, 0:src.shape[1], 0:src.shape[2]], src).then_inc(done, 16)
            for t in range(LAT // P):
                for half in range(2):
                    wait_evacuated(sp, ("out", t, half))
                sp.dma_start(out[0, t * P:(t + 1) * P, :], out_sb[:, t, :]).then_inc(out_stored, 16)
            sp.wait_ge(out_stored, 16 * (LAT // P))


ROW_DMAS = 12
LAST_SUB = 3
SUBLN_AT = [4 * h + 7 for h in range(DIFF_HEADS)]


def split_job(key):
    if key[0] in ("gate", "down", "qkv", "gdn"):
        return key
    return ("y", 0 if key[0] == "attout" else 2, key[1])


_INS = ['x', 'c', 'ctx', 'c_ctx', 'ada_w', 'ada_b', 'norm_g', 'attn_w_in', 'attn_w_out', 'diff_lambda',
        'diff_subln_g', 'gqa_qk_g', 'gdn_w_in', 'gdn_conv_w', 'gdn_a_log', 'gdn_dt_bias', 'gdn_norm_g',
        'gdn_w_out', 'ffn_w_gate_up', 'ffn_w_down']


def kernel(**inputs):
    import numpy as _np
    import concourse.bacc as _bacc
    from concourse import mybir as _mybir
    from concourse.bass_utils import run_bass_kernel_spmd as _run

    nc = _bacc.Bacc("TRN2", target_bir_lowering=False, num_devices=1)
    arrays, args = {}, []
    given = [(name, _np.ascontiguousarray(inputs[name])) for name in _INS]
    for name, a in given + [("tables", shape_tables()), ("levels", level_tables())]:
        arrays[f"in_{name}"] = a
        args.append(nc.dram_tensor(f"in_{name}", a.shape, _mybir.dt.from_np(a.dtype), kind="ExternalInput").ap())
    args.append(nc.dram_tensor("out_0", (1, LAT, D), F32, kind="ExternalOutput").ap())
    backbone(nc, *args)
    r = _run(nc, [arrays], core_ids=[0])
    return r.results[0]["out_0"]
```

```python
from contextlib import ExitStack

import numpy as np

import concourse.bass as bass
from concourse import mybir

F32 = mybir.dt.float32
F32R = mybir.dt.float32r
BF16 = mybir.dt.bfloat16
ALU = mybir.AluOpType
ACT = mybir.ActivationFunctionType
AXIS_X = mybir.AxisListType.X

P = 128
D = 1024
KT = D // P
CTX, LAT = 256, 256
T = CTX + LAT
STREAMS = ((0, CTX), (CTX, T))
GRID_W = 64
ROPE_THETA = 10000.0
RMS_EPS = 1e-6
HEAD = 64
DIFF_HEADS = 4
GQA_HEADS = 8
GQA_KV = 2
DQ_COL, DK_COL, DV_COL, GQ_COL, GK_COL, GV_COL = 0, 512, 1024, 1536, 2048, 2176
LAM_INIT = 0.8 - 0.6 * 1.0
GDN_SCALE = 128 ** -0.5
FFN = 2816
FT = FFN // P
GH = 8
GW = GH * P
CHUNK = 128
LEVELS = 7

C_IDENT, C_ONES, C_BLOCK, C_ROT = 0, 128, 256, 384
C_COS, C_SIN = 512, 768
C_TRIF, C_TRIB = 1024, 1152
C_HALF = 1280
C_EPS = 1282
C_ONE = 1283
C_FOLD = 1284
C_N = 1286

R_NORM, R_C, R_SUB, R_GDN, R_QKG, R_N = 0, 64, 80, 81, 82, 84


def shape_tables():
    t = np.zeros((P, C_N), np.float32)
    i = np.arange(P)
    t[i, C_IDENT + i] = 1
    t[:, C_ONES:C_ONES + P] = 1
    t[:, C_BLOCK:C_BLOCK + P] = (i[:, None] // HEAD == i[None, :] // HEAD)
    q = (i % 32) // 16
    low, high = i[q == 0], i[q == 1]
    t[low + 16, C_ROT + low] = -1
    t[high - 16, C_ROT + high] = 1
    n = np.arange(LAT)
    freq = ROPE_THETA ** (-np.arange(0, HEAD // 2, 2, dtype=np.float32) / np.float32(HEAD // 2))
    rows, cols = (n // GRID_W).astype(np.float32), (n % GRID_W).astype(np.float32)
    d = i % HEAD
    ang = np.where((d < HEAD // 2)[:, None], rows[None, :], cols[None, :]) * freq[d % 16][:, None]
    t[:, C_COS:C_COS + LAT] = np.cos(ang)
    t[:, C_SIN:C_SIN + LAT] = np.sin(ang)
    t[:, C_TRIF:C_TRIF + P] = (i[:, None] <= i[None, :])
    t[:, C_TRIB:C_TRIB + P] = (i[:, None] >= i[None, :])
    t[:HEAD, C_HALF] = HEAD ** -0.5
    t[HEAD:, C_HALF + 1] = HEAD ** -0.5
    t[:, C_EPS] = RMS_EPS
    t[:, C_ONE] = 1
    t[[0, 2], C_FOLD] = 1
    t[[1, 3], C_FOLD + 1] = 1
    return t


def level_tables():
    i = np.arange(P)
    m = np.zeros((P, LEVELS, 3, P), np.float32)
    for n in range(LEVELS):
        s = 1 << n
        row, col = i[:, None], i[None, :]
        low = (row // (2 * s) == col // (2 * s)) & (row // s % 2 == 1) & (col // s % 2 == 0)
        m[:, n, 0], m[:, n, 1], m[:, n, 2] = low, low.T, low
    return m.reshape(P, LEVELS * 3 * P)


ADA_WIDTH = 512
ADA_TILES = 2
ADA_ROUNDS = KT // ADA_TILES
ADA_GROUPS = 6 * D // ADA_WIDTH
ADA_N = 2 * ADA_GROUPS * ADA_ROUNDS
QKV_STEPS = ([("gk", 0), ("gv", 0)] + [("dk", t) for t in range(4)] + [("dv", t) for t in range(4)]
             + [("dq", t) for t in range(4)] + [("gq", t) for t in range(4)])
ATT_UNITS = [(head, qb) for head in range(DIFF_HEADS + GQA_HEADS) for qb in range(T // P)]
QK_TILES = [s for s in QKV_STEPS if s[0] not in ("gv", "dv")]
V_TILES = [s for s in QKV_STEPS if s[0] in ("gv", "dv")]
NORMED = [u for u, s in enumerate(QK_TILES) if s[0] in ("gk", "gq")]
GDN_STEPS = ([("ab", 0)] + [("k", h) for h in range(GH)] + [("v", h) for h in range(GH)]
             + [("q", h) for h in range(GH)] + [("z", h) for h in range(GH)])
CONV_TILES = [s for s in GDN_STEPS if s[0] in "kvq"]
CONV_CHANNEL = {"q": 0, "k": GH, "v": 2 * GH}
SCALED_BY_VECTOR = {"pre": (1, 4), "post": (1, 3, 6)}
DOWN_PARTS = ((0, 8), (8, 16), (16, FT))


def stat_at(n):
    return [u for u in NORMED if QKV_STEPS.index(QK_TILES[u]) == n - 1]


def rotate_at(n):
    return [u for u, s in enumerate(QK_TILES) if QKV_STEPS.index(s) == n - (2 if u in NORMED else 1)]


def maps_of(head):
    if head < DIFF_HEADS:
        return [(head, 0, 1 + head), (head, 1, 1 + head)]
    g, r = divmod(head - DIFF_HEADS, GQA_HEADS // GQA_KV)
    return [(DIFF_HEADS + r, g, 0)]


def map_no(n, m):
    pairs = min(n, DIFF_HEADS * 4)
    return n + pairs + m


def keys_of(qb):
    return T if qb >= CTX // P else CTX


def scan_chunk(d, step):
    return step if d == 0 else (1, 0, 3, 2)[step]


def ada_after(phase, step):
    if phase == "start":
        return list(range(16))
    if phase == "qkv":
        return [16 + step]
    if phase == "att" and step % 3 == 2 and step // 3 < 14:
        return [34 + step // 3]
    if phase == "gate0":
        return [48 + step]
    if phase == "down0" and 0 <= step < 4:
        return [92 + step]
    return []


def ada_turns(n):
    flush = (ada_after("start", 0)[-1], ADA_N - 1)
    before = [n // ADA_ROUNDS - 1] if n % ADA_ROUNDS == 0 and n and n - 1 not in flush else []
    return before, [n // ADA_ROUNDS] if n in flush else []


def stream():
    out = [("ada", n) for n in ada_after("start", 0)]
    for n, (kind, t) in enumerate(QKV_STEPS):
        out += [("qkv", kind, t)] + [("ada", a) for a in ada_after("qkv", n)]
    for n in range(len(ATT_UNITS)):
        out += [("ada", a) for a in ada_after("att", n)]
    out += [("attout", m) for m in range(KT)]
    for layer in range(2):
        if layer:
            out += [("gdn", kind, t) for kind, t in GDN_STEPS] + [("gdnout", m) for m in range(KT)]
        for n in range(2 * FT):
            out += [("gate", layer, n)] + [("ada", a) for a in ada_after(f"gate{layer}", n)]
        for m in range(KT):
            out += [("down", layer, m, part) for part in range(3)]
            out += [("ada", a) for a in ada_after(f"down{layer}", m)]
    return out


def backbone(nc, x, c, ctx, c_ctx, ada_w, ada_b, norm_g, attn_w_in, attn_w_out, diff_lambda,
             diff_subln_g, gqa_qk_g, gdn_w_in, gdn_conv_w, gdn_a_log, gdn_dt_bias, gdn_norm_g,
             gdn_w_out, ffn_w_gate_up, ffn_w_down, tables, levels, out):
    with ExitStack() as stack:
        def sem(name):
            return stack.enter_context(nc.semaphore(name))

        top = [(nc.sbuf_base + 31) // 32 * 32]

        def at(name, shape, dtype, offset):
            return nc.alloc_sbuf_tensor_at(name, [P] + shape, dtype, offset=offset)[:]

        def place(name, shape, dtype=F32):
            size = int(np.prod(shape)) * (2 if dtype == BF16 else 4)
            offset = top[0]
            top[0] += (size + 31) // 32 * 32
            return at(name, shape, dtype, offset)

        N_RAW, N_SPLIT = 8, 3
        xT = place("xT", [KT, T])
        H_BASE = top[0]
        h_hi = place("h_hi", [KT, T], F32R)
        h_lo = place("h_lo", [KT, T], F32R)
        W_BASE = top[0]
        h_work = at("h_work", [KT, T], F32, H_BASE + KT * T * 4)
        w_raw = [place(f"w_raw{n}", [KT, P]) for n in range(N_RAW)]
        w_lo = [at(f"w_lo{n}", [KT, P], F32R, W_BASE + n * KT * P * 4) for n in range(N_RAW)]
        W_HI_BASE = top[0]
        w_hi = [place(f"w_hi{n}", [KT, P], F32R) for n in range(N_SPLIT)]
        BIG = top[0]
        top[0] += FT * T * 4 * 2
        scr = top[0]
        top[0] += 8448
        tab = place("tab", [C_N])
        level_mask = place("level_mask", [LEVELS, 3, P], BF16)
        colsA = place("colsA", [R_N])
        ada_bias = place("ada_bias", [2 * 6 * KT])
        conv_cols = place("conv_cols", [4 * 3 * GH])
        silu_c = place("silu_c", [KT, 2])
        silu_split = place("silu_split", [KT, 4], F32R)
        ada_rows = place("ada_rows", [ADA_WIDTH])
        mods = place("mods", [2, 6, KT, 2])
        lam_row = place("lam_row", [4 * HEAD])
        lam_two = place("lam_two", [5])
        dt_row = place("dt_row", [2 * GH])
        alog_row = place("alog_row", [2 * GH])
        gates = place("gates", [10, 4, 2 * GH])
        stats = place("stats", [4, 6])
        sub_gain = place("sub_gain", [1])
        el = place("el", [2, 4, 4])
        wl = place("wl", [2, 4, 4])
        assert top[0] <= nc.sbuf_usable_end, (top[0], nc.sbuf_usable_end)

        ident, ones = tab[:, C_IDENT:C_IDENT + P], tab[:, C_ONES:C_ONES + P]
        block_ones, rotation = tab[:, C_BLOCK:C_BLOCK + P], tab[:, C_ROT:C_ROT + P]
        cosT, sinT = tab[:, C_COS:C_COS + LAT], tab[:, C_SIN:C_SIN + LAT]
        tri = [tab[:, C_TRIF:C_TRIF + P], tab[:, C_TRIB:C_TRIB + P]]
        eps, one = tab[:, C_EPS:C_EPS + 1], tab[:, C_ONE:C_ONE + 1]

        tok = at("tok", [4, D], F32, BIG)
        rowsA = at("rowsA", [P], F32, BIG + 16384)
        rowsB = at("rowsB", [P], F32, BIG + 16896)
        rowsC = at("rowsC", [P], F32, BIG + 17408)
        level_f32 = at("level_f32", [LEVELS * 3 * P], F32, BIG + 18432)
        act_hi = at("act_hi", [FT, T], F32R, BIG)
        act_lo = at("act_lo", [FT, T], F32R, BIG + FT * T * 4)
        q_sb = at("q_sb", [KT, 2, T], F32, BIG)
        k_sb = at("k_sb", [5, T], F32, BIG + 32768)
        v_sb = at("v_sb", [4, 768], F32, BIG + 43008)
        probs = at("probs", [3, 2, T], F32, BIG + 55296)
        probsT = at("probsT", [2, 4, P], F32, BIG + 67584)
        o_sb = at("o_sb", [KT, T], F32, BIG + 71680)
        o_sq = at("o_sq", [T], F32, BIG + 88064)
        qk_n = at("qk_n", [3, T], F32, BIG + 71680)
        qk_sq = at("qk_sq", [2, T], F32, BIG + 77824)
        qk_cosed = at("qk_cosed", [2, LAT], F32, BIG + 81920)
        qk_sined = at("qk_sined", [2, LAT], F32, BIG + 83968)
        v_fm = at("v_fm", [2, T], F32, BIG + 86016)
        s_tmp = at("s_tmp", [2, T], F32, scr)
        a_tmp = at("a_tmp", [2, T], F32, scr + 4096)

        k_fm = at("k_fm", [GH, T], F32, BIG)
        k_tok = at("k_tok", [4, GH, P], F32, BIG + 16384)
        v_tok = at("v_tok", [4, GH, P], F32, BIG + 32768)
        q_fm = at("q_fm", [GH, LAT], F32, BIG + 49152)
        z_fm = at("z_fm", [GH, LAT], F32, BIG + 57344)
        o_fm = at("o_fm", [GH, LAT], F32, BIG + 65536)
        u_odd = at("u_odd", [4, 4, P], F32, BIG + 73728)
        attnT = at("attnT", [2, 4, P], F32, BIG + 81920)
        q_dec = at("q_dec", [2, 4, P], F32, BIG + 86016)
        gdn_sq = at("gdn_sq", [2, T], F32, BIG + 73728)
        read_squares = at("read_squares", [2, LAT], F32, BIG + 81920)
        read_t = at("read_t", [2, LAT], F32, BIG + 86016)
        conv_in = [at(f"conv_in{n}", [2, CTX + 3], F32, scr + 2080 * n) for n in range(2)]
        conv_out = [at(f"conv_out{n}", [T], F32, scr + 4160 + 2048 * n) for n in range(2)]
        masked_w = at("masked_w", [2, 4, P], F32, scr + 4096)
        row_decay = at("row_decay", [2, 4, P], F32, scr)
        h_area = [[at(f"h_area{n}_{m}", [4, P], F32, H_BASE + 8192 * n + 2048 * m) for m in range(4)]
                  for n in range(4)]
        n_mat = [h_area[c][0] for c in range(4)]
        t_mat = [h_area[c][1] for c in range(4)]
        u_even = [h_area[c][2] for c in range(4)]
        z_mat = [h_area[c][3] for c in range(4)]
        state, scan_rhs, v_new, v_end = [at(name, [4, P], F32, W_HI_BASE + 2048 * m) for m, name in
                                         enumerate(("state", "scan_rhs", "v_new", "v_end"))]
        v_beta = at("v_beta", [2, 4, P], F32, W_HI_BASE + 8192)

        def norm_views(name, offset):
            return (at(name + "_rstd", [T], F32, offset), at(name + "_sq", [4, T], F32, offset + 2048),
                    at(name + "_acc", [T], F32, offset + 10240))

        pre_rstd, pre_sq, _ = norm_views("pre", BIG + 73728)
        post_views = [norm_views("post0", BIG + 73728), norm_views("post1", H_BASE + 16384),
                      norm_views("post2", BIG + 73728), norm_views("post3", H_BASE + 16384)]
        y_views = [at("y0", [KT, T], F32, BIG), at("y1", [KT, T], F32, H_BASE),
                   at("y2", [KT, T], F32, BIG), at("y3", [KT, T], F32, H_BASE)]
        out_sb = at("out_sb", [2, D], F32, BIG)

        banks = [stack.enter_context(nc.psum_tensor(f"bank{n}", [P, T], F32))[:] for n in range(8)]
        RINGS = {"work": (2, 3, 4, 5, 6), "side": (7, 1)}
        taken = {"work": 0, "side": 0}
        used = [0] * 8
        turn_of = {}
        done_at = {}

        products_done = sem("products_done")
        evacuated = [sem(f"evacuated{n}") for n in range(8)]
        raw_in = [sem(f"raw_in{n}") for n in range(N_RAW)]
        w_hi_ready, w_lo_ready = sem("w_hi_ready"), sem("w_lo_ready")
        tables_in, rows_in, tok_in = sem("tables_in"), sem("rows_in"), sem("tok_in")
        levels_in, levels_ready = sem("levels_in"), sem("levels_ready")
        act_chain, dve_chain, pool_chain = sem("act_chain"), sem("dve_chain"), sem("pool_chain")
        silu_ready, silu_split_ready = sem("silu_ready"), sem("silu_split_ready")
        lam_sums, lam_exps, lam_ready = sem("lam_sums"), sem("lam_exps"), sem("lam_ready")
        rows_ready, mods_ready = sem("rows_ready"), sem("mods_ready")
        pre_sq_ready = sem("pre_sq_ready")
        scaled = {(norm, on_vector): sem(f"{norm}_scaled_{'vector' if on_vector else 'gpsimd'}")
                  for norm in ("pre", "post") for on_vector in (False, True)}
        h32_ready, h_ready = sem("h32_ready"), sem("h_ready")
        y_acc_ready, x_updated = sem("y_acc_ready"), sem("x_updated")
        qk_normed, qk_cos, qk_roped, qk_out = sem("qk_normed"), sem("qk_cos"), sem("qk_roped"), sem("qk_out")
        max_ready, probs_ready, o_scaled = sem("max_ready"), sem("probs_ready"), sem("o_scaled")
        o_hi_ready, o_lo_ready = sem("o_hi_ready"), sem("o_lo_ready")
        act_hi_ready, act_lo_ready = sem("act_hi_ready"), sem("act_lo_ready")
        pads_ready = sem("pads_ready")
        conv_done, conv_silu = sem("conv_done"), sem("conv_silu")
        gate_pre, gate_exp, gate_sp, gate_ready = sem("gate_pre"), sem("gate_exp"), sem("gate_sp"), sem("gate_ready")
        gate_decay = sem("gate_decay")
        norm_sq, normed = sem("norm_sq"), sem("normed")
        tri_gates, diffs_ready = sem("tri_gates"), sem("diffs_ready")
        attn_raw, attn_ready, u_ready, vb_ready = sem("attn_raw"), sem("attn_ready"), sem("u_ready"), sem("vb_ready")
        z_ready = sem("z_ready")
        read_sq, read32 = sem("read_sq"), sem("read32")
        out_stored = sem("out_stored")

        chunks = stream()
        if LAST_SUB < 2:
            chunks = [k for k in chunks if k[0] == "ada" or k[0] in ("qkv", "attout") or k[1] == 0]
        where = {key: n for n, key in enumerate(chunks)}
        FIRST_CHUNK = [("qkv", "gk", 0), ("gate", 0, 0), ("gdn", "ab", 0), ("gate", 1, 0)]

        landed = []
        for n, key in enumerate(chunks):
            landed.append((landed[n - N_RAW] if n >= N_RAW else 0) + 16 * (2 if key[:2] == ("qkv", "gq") else 1))

        def raw_slot(key):
            return w_raw[where[key] % N_RAW]

        def wait_raw(eng, key):
            eng.wait_ge(raw_in[where[key] % N_RAW], landed[where[key]])

        def wait_product(eng, job):
            eng.wait_ge(products_done, done_at[job])

        def wait_evacuated(eng, job):
            bank, turn = turn_of[job]
            eng.wait_ge(evacuated[bank], turn)

        def release(ins, job):
            ins.then_inc(evacuated[turn_of[job][0]], 1)

        def bank(job):
            return banks[turn_of[job][0]]

        def chunk_shape(key):
            if key[0] == "down":
                a, b = DOWN_PARTS[key[3]]
                return b - a, P
            return KT, 2 * 2 * GH if key[:2] == ("gdn", "ab") else P

        def mod_col(layer, part, k, s):
            return mods[:, layer, part, k, s:s + 1]

        def first_token(i):
            return 0 if i < 3 else CTX

        def first_out(i):
            return 0 if i < 2 else CTX

        def scaled_tiles(norm, on_vector):
            return [k for k in range(KT) if (k in SCALED_BY_VECTOR[norm]) == on_vector]

        def wait_scaled(eng, norm, i, k):
            on_vector = k in SCALED_BY_VECTOR[norm]
            tiles = scaled_tiles(norm, on_vector)
            eng.wait_ge(scaled[norm, on_vector], i * len(tiles) + tiles.index(k) + 1)

        def scale_pre(eng, i, k, on_vector):
            lo = first_token(i)
            if k == scaled_tiles("pre", on_vector)[0]:
                wait_evacuated(eng, ("pre", i))
            (nc.vector if on_vector else nc.gpsimd).tensor_tensor(
                h_work[:, k, lo:T], xT[:, k, lo:T], pre_rstd[:, lo:T],
                ALU.mult).then_inc(scaled["pre", on_vector], 1)

        def scale_post(eng, i, k, on_vector):
            lo = first_out(i)
            if k == scaled_tiles("post", on_vector)[0]:
                wait_evacuated(eng, ("post", i))
            (nc.vector if on_vector else nc.gpsimd).tensor_tensor(
                y_views[i][:, k, lo:T], y_views[i][:, k, lo:T], post_views[i][0][:, lo:T],
                ALU.mult).then_inc(scaled["post", on_vector], 1)

        def x_ready(eng, i, k):
            if i == 0:
                wait_evacuated(eng, ("x", k))
            else:
                eng.wait_ge(x_updated, (i - 1) * KT + k + 1)

        def units(ap):
            return ap.rearrange("p (u n) -> p u n", n=P)

        def both(ap):
            return ap.unsqueeze(2).to_broadcast([P, 2, 2, P])

        HEAD_PAIRS = GH // 2
        CHUNKS = T // CHUNK
        LAT_CHUNK = CTX // CHUNK
        SCAN_FROM, SCAN_EARLY = 8, 4
        CONV_LAG = 2
        NORM_FROM = len(CONV_TILES) + 3

        def conv_step(n):
            return CONV_TILES.index(GDN_STEPS[n]) if 0 <= n < len(GDN_STEPS) and GDN_STEPS[n] in CONV_TILES else None

        def conv_lo(u):
            return CTX if CONV_TILES[u][0] == "q" else 0

        def norm_tile(e):
            return (k_fm[:, e, :], T) if e < GH else (q_fm[:, e - GH, :], LAT)

        def gate_cols(ap, c, unit, p):
            col = unit // 2 * GH + 2 * p + unit % 2
            return ap[:, c, col:col + 1]

        log_decay, beta_g, cum_g, neg_decay, neg_cum = [gates[:, n] for n in (3, 5, 6, 7, 8)]

        def end_col(d):
            return CHUNK - 1 if d == 0 else 0

        def attn_of(p, c, units):
            return xT[:, units, c * P:(c + 1) * P] if p % 2 else attnT[:, c, units, :]

        def u_of(p, c):
            return u_odd[:, c] if p % 2 else u_even[c]

        def q_dec_of(p, c, units):
            shifted = slice(units.start + 4, units.stop + 4)
            return xT[:, shifted, c * P:(c + 1) * P] if p % 2 else q_dec[:, c, units, :]

        def core_steps(p):
            build, scan = [], []
            if p < HEAD_PAIRS:
                ahead = 2
                for c in range(CHUNKS + ahead):
                    build += [("R", p, c)] * (c < CHUNKS) + [("G", p, c - ahead)] * (c >= ahead)
                build += [("NT", p, c) for c in range(CHUNKS)]
                for level in range(1, LEVELS):
                    build += [(job, p, level, c) for job in ("Z", "TT", "W") for c in range(CHUNKS)]
            if p:
                for step in range(CHUNKS):
                    scan += [(job, p - 1, step) for job, there in
                             (("KS", step > 0), ("VN", True), ("O", step >= LAT_CHUNK), ("S", step < CHUNKS - 1))
                             if there]
            if not build:
                for n, h in enumerate(readout_heads(p)):
                    scan.insert(2 * n + 1, ("osum", h))
                return scan
            out, early = [], (SCAN_FROM, SCAN_FROM + SCAN_EARLY)
            every = (len(build) - early[1]) // (len(scan) - SCAN_EARLY + 1)
            for n, job in enumerate(build):
                if n >= early[0] and scan and (n < early[1] or (n - early[1]) % every == every - 1):
                    out.append(scan.pop(0))
                out.append(job)
            assert not scan
            return out

        def readout_heads(p):
            return range(0, 2 * (HEAD_PAIRS - 1)) if p == HEAD_PAIRS else range(2 * (HEAD_PAIRS - 1), GH)

        def norm_parts(n):
            bounds = (0, 2, 4, 7, 10, 13, 16, 2 * GH + 2)
            return range(*bounds[n - NORM_FROM:][:2]) if n >= NORM_FROM else []

        def build_no(p, level, c):
            return (p * LEVELS + level) * CHUNKS + c

        def gdn_tensor(pe, take, finish, project, to_tokens):
            def step(n):
                kind, h = GDN_STEPS[n]
                key = ("gdn", kind, h)
                project(key, key, CTX if kind in "qz" else 0, 2 if n == 0 else None, chunk_shape(key)[1])
                if n == 1:
                    wait_evacuated(pe, ("gdn", "ab", 0))
                    to_tokens(("ab_turned", 0), conv_out[1][0:4 * GH, :])
                if n == 4:
                    pe.wait_ge(gate_sp, 1)
                    dst = take(("cum", 0), "side")
                    for c in range(CHUNKS):
                        for d in range(2):
                            a = c * 2 * GH + d * GH
                            m = nc.tensor.matmul(dst[:, a:a + GH], tri[d], log_decay[:, c, d * GH:(d + 1) * GH],
                                                 start=True, stop=True)
                    finish(m, ("cum", 0))

            for n in range(len(GDN_STEPS) + 1):
                if n < len(GDN_STEPS):
                    step(n)
                u = conv_step(n - CONV_LAG)
                if u is not None and CONV_TILES[u][0] == "v":
                    pe.wait_ge(conv_silu, u + 1)
                    h = CONV_TILES[u][1]
                    dst = take(("vt", h))
                    for c in range(CHUNKS):
                        m = nc.tensor.transpose(dst[:, c * P:(c + 1) * P], conv_out[u % 2][:, c * P:(c + 1) * P], ident)
                    finish(m, ("vt", h))
                for e in norm_parts(n):
                    if e < 2 * GH:
                        pe.wait_ge(norm_sq, e + 1)
                        width = norm_tile(e)[1]
                        dst = take(("ksum", e), "side")
                        finish(nc.tensor.matmul(dst[:, 0:width], ones, gdn_sq[:, e % 2, 0:width], start=True,
                                                stop=True), ("ksum", e))
                    if 2 <= e < GH + 2:
                        pe.wait_ge(normed, e - 1)
                        to_tokens(("kt", e - 2), k_fm[:, e - 2, :])

            def read_head(h):
                pe.wait_ge(read_sq, h + 1)
                finish(nc.tensor.matmul(take(("osum", h), "side")[:, 0:LAT], ones, read_squares[:, h % 2, :],
                                        start=True, stop=True), ("osum", h))

            for job in [job for p in range(HEAD_PAIRS + 1) for job in core_steps(p)]:
                kind, p, c = job[0], job[1], job[-1]
                if kind == "osum":
                    read_head(p)
                    continue
                if kind == "R":
                    pe.wait_ge(tri_gates, p * CHUNKS + c + 1)
                    m = nc.tensor.matmul(take(job, "side" if c < 2 else "work"), ones,
                                         n_mat[c].rearrange("p u n -> p (u n)"), start=True, stop=True)
                elif kind == "G":
                    if p == 0 and c == 0:
                        pe.wait_ge(normed, 2 * GH)
                    dst = take(job)
                    span = slice(c * CHUNK, (c + 1) * CHUNK)
                    lat = slice((c - LAT_CHUNK) * CHUNK, (c - LAT_CHUNK + 1) * CHUNK)
                    for hh in range(2):
                        k_c = k_fm[:, 2 * p + hh, span]
                        m = nc.tensor.matmul(dst[:, hh * P:(hh + 1) * P], k_c, k_c, start=True, stop=True)
                    if c >= LAT_CHUNK:
                        for hh in range(2):
                            m = nc.tensor.matmul(dst[:, (2 + hh) * P:(3 + hh) * P], k_fm[:, 2 * p + hh, span],
                                                 q_fm[:, 2 * p + hh, lat], start=True, stop=True)
                elif kind in ("NT", "TT"):
                    if kind == "NT":
                        wait_evacuated(pe, ("G", p, c))
                    else:
                        pe.wait_ge(u_ready, build_no(p, job[2] - 1, c) + 1)
                    src = n_mat[c] if kind == "NT" else u_of(p, c)
                    dst = take(job)
                    for unit in range(4):
                        m = nc.tensor.transpose(dst[:, unit * P:(unit + 1) * P], src[:, unit, :], ident)
                elif kind in ("Z", "W"):
                    if kind == "Z":
                        pe.wait_ge(u_ready, build_no(p, job[2] - 1, c) + 1)
                    else:
                        wait_evacuated(pe, ("Z",) + job[1:])
                        wait_evacuated(pe, ("TT",) + job[1:])
                    left, right = (n_mat[c], u_of(p, c)) if kind == "Z" else (t_mat[c], z_mat[c])
                    dst = take(job)
                    for unit in range(4):
                        m = nc.tensor.matmul(dst[:, unit * P:(unit + 1) * P], left[:, unit, :], right[:, unit, :],
                                             start=True, stop=True)
                else:
                    s = c
                    cc = [scan_chunk(unit // 2, s) for unit in range(4)]
                    if kind == "KS":
                        wait_evacuated(pe, ("S", p, s - 1))
                    elif kind == "VN" and s:
                        wait_evacuated(pe, ("KS", p, s))
                    elif kind == "VN":
                        pe.wait_ge(u_ready, (p + 1) * LEVELS * CHUNKS)
                        pe.wait_ge(vb_ready, p * CHUNKS + 1)
                    else:
                        wait_evacuated(pe, ("VN", p, s))
                    if kind == "O":
                        pe.wait_ge(attn_ready, (p + 1) * (CHUNKS - LAT_CHUNK))
                    dst = take(job)
                    for unit in range(4):
                        part, h = dst[:, unit * P:(unit + 1) * P], 2 * p + unit % 2
                        if kind == "KS":
                            m = nc.tensor.matmul(part, k_fm[:, h, cc[unit] * CHUNK:(cc[unit] + 1) * CHUNK],
                                                 state[:, unit, :], start=True, stop=True)
                        elif kind == "VN":
                            rhs = scan_rhs[:, unit, :] if s else v_beta[:, 0, unit, :]
                            m = nc.tensor.matmul(part, u_of(p, cc[unit])[:, unit, :], rhs, start=True, stop=True)
                        elif kind == "S":
                            m = nc.tensor.matmul(part, k_tok[:, cc[unit], h, :], v_end[:, unit, :],
                                                 start=True, stop=True)
                        else:
                            one_unit = slice(unit, unit + 1)
                            nc.tensor.matmul(part, state[:, unit, :], q_dec_of(p, cc[unit] - LAT_CHUNK, one_unit)[:, 0],
                                             start=True, stop=False)
                            m = nc.tensor.matmul(part, v_new[:, unit, :], attn_of(p, cc[unit] - LAT_CHUNK, one_unit)[:, 0],
                                                 start=False, stop=True)
                finish(m, job)
            for h in readout_heads(HEAD_PAIRS + 1):
                read_head(h)

        def gdn_scalar(act, link, split_to, rstd, preload_logs):
            def square(e):
                tile, width = norm_tile(e)
                if e >= 2:
                    act.wait_ge(normed, e - 1)
                act.wait_ge(conv_silu, len(CONV_TILES))
                nc.scalar.activation(gdn_sq[:, e % 2, 0:width], tile, ACT.Square).then_inc(norm_sq, 1)

            act.wait_ge(pads_ready, 1)
            for n in range(len(GDN_STEPS) + 1):
                if n < len(GDN_STEPS):
                    kind, h = GDN_STEPS[n]
                    key = ("gdn", kind, h)
                    split_to(min(where[key] + 2, where[("gdn", "z", GH - 1)]))
                    wait_product(act, key)
                    if kind == "ab":
                        release(nc.scalar.activation(conv_out[1][0:4 * GH, :], bank(key)[0:4 * GH, :], ACT.Copy), key)
                        job = ("ab_turned", 0)
                        act.wait_ge(gate_pre, 1)
                        b = bank(job)[:, 0:16 * GH].rearrange("p (c n) -> p c n", c=CHUNKS)[:, :, 2 * GH:4 * GH]
                        release(nc.scalar.activation(beta_g, b, ACT.Sigmoid), job)
                        link(nc.scalar.activation(gates[:, 2], gates[:, 2], ACT.Exp))
                        nc.scalar.activation(alog_row, alog_row, ACT.Exp)
                        nc.scalar.activation(gates[:, 2], gates[:, 2], ACT.Ln, bias=one).then_inc(gate_exp, 1)
                    elif kind == "z":
                        release(nc.scalar.activation(z_fm[:, h, :], bank(key)[:, CTX:T], ACT.Copy), key)
                    else:
                        u = CONV_TILES.index((kind, h))
                        if u >= 2:
                            act.wait_ge(conv_done, u - 1)
                        lo = conv_lo(u)
                        release(nc.scalar.activation(conv_in[u % 2][:, lo // CTX:2, 2:2 + CTX],
                                                     bank(key)[:, lo:T].rearrange("p (s n) -> p s n", n=CTX),
                                                     ACT.Copy), key)
                u = conv_step(n - 1)
                if u is not None:
                    act.wait_ge(conv_done, u + 1)
                    kind, h = CONV_TILES[u]
                    dst = {"k": k_fm[:, h, :], "q": q_fm[:, h, :], "v": conv_out[u % 2]}[kind]
                    nc.scalar.activation(dst, conv_out[u % 2][:, conv_lo(u):T], ACT.Silu).then_inc(conv_silu, 1)
                if n == 6:
                    wait_evacuated(act, ("cum", 0))
                    nc.scalar.activation(neg_decay, cum_g, ACT.Exp).then_inc(gate_decay, 1)
                if n == NORM_FROM:
                    preload_logs()
                    square(0)
                for e in norm_parts(n):
                    if e + 1 < 2 * GH:
                        square(e + 1)
                    if e < 2 * GH:
                        width = norm_tile(e)[1]
                        rstd(gdn_sq[:, e % 2, 0:width], bank(("ksum", e))[:, 0:width], ("ksum", e), 1.0)
                    if 2 <= e < GH + 2:
                        wait_product(act, ("kt", e - 2))
                        release(nc.scalar.activation(k_tok[:, :, e - 2, :], units(bank(("kt", e - 2))), ACT.Copy),
                                ("kt", e - 2))

            def read_head(h):
                if h == 0:
                    head_squares(0)
                if h + 1 < GH and h + 1 != readout_heads(HEAD_PAIRS).stop:
                    head_squares(h + 1)
                rstd(read_squares[:, h % 2, :], bank(("osum", h))[:, 0:LAT], ("osum", h), 1.0 / P)

            def head_squares(h):
                if h >= 2:
                    act.wait_ge(read32, h - 1)
                wait_evacuated(act, ("O", h // 2, CHUNKS - 1))
                nc.scalar.activation(read_squares[:, h % 2, :], o_fm[:, h, :], ACT.Square).then_inc(read_sq, 1)

            for p in range(HEAD_PAIRS + 1):
                if p == HEAD_PAIRS:
                    nc.scalar.activation(z_fm, z_fm, ACT.Silu).then_inc(z_ready, 1)
                    preload_logs()
                for job in core_steps(p):
                    kind, q, c = job[0], job[1], job[-1]
                    if kind == "osum":
                        read_head(q)
                    elif kind == "R":
                        act.wait_ge(diffs_ready, p * CHUNKS + c + 1)
                        rows = units(bank(job))
                        for unit in range(4):
                            last = nc.scalar.activation(t_mat[c][:, unit, :], rows[:, unit, :], ACT.Relu,
                                                        bias=gate_cols(neg_cum, c, unit, p))
                        link(last)
                        nc.scalar.activation(t_mat[c], t_mat[c], ACT.Exp, scale=-1.0)
                        nc.scalar.activation(u_of(p, c), u_of(p, c), ACT.Exp)
                        if c >= LAT_CHUNK:
                            if p:
                                act.wait_ge(attn_ready, (p - 1) * (CHUNKS - LAT_CHUNK) + c - LAT_CHUNK + 1)
                            nc.scalar.activation(row_decay[:, c - LAT_CHUNK], rows, ACT.Exp)
                        for d in range(2):
                            last = nc.scalar.activation(el[:, p % 2, c, 2 * d:2 * d + 2],
                                                        rows[:, 2 * d:2 * d + 2, end_col(d)], ACT.Exp)
                        release(last, job)
                    elif kind in ("Z", "TT"):
                        wait_product(act, job)
                        if job[2] > 1:
                            wait_product(act, ("W", p, job[2] - 1, c))
                        release(nc.scalar.activation((z_mat if kind == "Z" else t_mat)[c], units(bank(job)), ACT.Copy),
                                job)
                    elif kind == "VN":
                        wait_product(act, job)
                        nc.scalar.activation(v_new, units(bank(job)), ACT.Copy)
                        cc = [scan_chunk(unit // 2, c) for unit in range(4)]
                        for unit in range(4):
                            last = nc.scalar.activation(v_end[:, unit, :], bank(job)[:, unit * P:(unit + 1) * P],
                                                        ACT.Copy, scale=wl[:, q % 2, cc[unit], unit:unit + 1])
                        release(last, job)
            head_squares(readout_heads(HEAD_PAIRS).stop)
            split_to(where[("gdnout", 0)] + 2)
            for h in readout_heads(HEAD_PAIRS + 1):
                read_head(h)

        def gdn_vector(dve, link, split_to):
            def read_head(h):
                wait_evacuated(dve, ("osum", h))
                if h == 0:
                    dve.wait_ge(z_ready, 1)
                if h >= 2:
                    dve.wait_ge(o_lo_ready, KT + h - 1)
                link(nc.vector.scalar_tensor_tensor(out=read_t[:, h % 2, :], in0=o_fm[:, h, :],
                                                    scalar=colsA[:, R_GDN:R_GDN + 1], in1=read_squares[:, h % 2, :],
                                                    op0=ALU.mult, op1=ALU.mult))
                nc.vector.tensor_tensor(read_t[:, h % 2, :], read_t[:, h % 2, :], z_fm[:, h, :],
                                        ALU.mult).then_inc(read32, 1)
                dve.wait_ge(read32, h + 1)
                nc.vector.tensor_copy(h_hi[:, h, CTX:T], read_t[:, h % 2, :]).then_inc(o_hi_ready, 1)

            for n in range(len(GDN_STEPS) + 1):
                if n < len(GDN_STEPS):
                    split_to(min(where[("gdn",) + GDN_STEPS[n]] + 2, where[("gdn", "z", GH - 1)]))
                u = conv_step(n - CONV_LAG)
                if u is not None and CONV_TILES[u][0] == "v":
                    h = CONV_TILES[u][1]
                    wait_product(dve, ("vt", h))
                    release(nc.vector.tensor_copy(v_tok[:, :, h, :], units(bank(("vt", h)))), ("vt", h))
                u = conv_step(n)
                if n == 0:
                    job = ("ab_turned", 0)
                    wait_product(dve, job)
                    rows = lambda ap: ap.unsqueeze(1).to_broadcast([P, CHUNKS, 2 * GH])
                    link(nc.vector.tensor_tensor(gates[:, 0], bank(job)[:, 0:16 * GH].rearrange(
                        "p (c n) -> p c n", c=CHUNKS)[:, :, 0:2 * GH], rows(dt_row), ALU.add))
                    nc.vector.tensor_scalar(gates[:, 1], gates[:, 0], 0.0, None, ALU.max)
                    link(nc.vector.tensor_scalar(gates[:, 2], gates[:, 0], -1.0, None, ALU.mult))
                    nc.vector.tensor_tensor(gates[:, 2], gates[:, 2], gates[:, 0], ALU.min).then_inc(gate_pre, 1)
                if n == 1:
                    dve.wait_ge(gate_exp, 1)
                    link(nc.vector.tensor_tensor(gates[:, 1], gates[:, 1], gates[:, 2], ALU.add))
                    nc.vector.scalar_tensor_tensor(out=log_decay, in0=gates[:, 1], scalar=-1.0,
                                                   in1=alog_row.unsqueeze(1).to_broadcast([P, CHUNKS, 2 * GH]),
                                                   op0=ALU.mult, op1=ALU.mult).then_inc(gate_sp, 1)
                if n == 5:
                    wait_product(dve, ("cum", 0))
                    release(nc.vector.tensor_copy(cum_g, bank(("cum", 0))[:, 0:CHUNKS * 2 * GH].rearrange(
                        "p (c n) -> p c n", c=CHUNKS)), ("cum", 0))
                if n == 8:
                    dve.wait_ge(gate_decay, 1)
                    nc.vector.tensor_scalar(neg_cum, cum_g, -1.0, None, ALU.mult)
                    nc.vector.scalar_tensor_tensor(out=neg_decay, in0=neg_decay, scalar=-1.0, in1=beta_g,
                                                   op0=ALU.mult, op1=ALU.mult).then_inc(gate_ready, 1)
                if u is not None:
                    kind, h = CONV_TILES[u]
                    wait_evacuated(dve, ("gdn", kind, h))
                    if u >= 2:
                        dve.wait_ge(conv_silu, u - 1)
                        if CONV_TILES[u - 2][0] == "v":
                            wait_product(dve, ("vt", CONV_TILES[u - 2][1]))
                    lo = conv_lo(u)
                    dst = conv_out[u % 2][:, lo:T].rearrange("p (s n) -> p s n", n=CTX)
                    src = conv_in[u % 2][:, lo // CTX:2, :]
                    tap = lambda j: conv_cols[:, (j * 3 * GH + CONV_CHANNEL[kind] + h):][:, 0:1]
                    link(nc.vector.tensor_scalar(dst, src[:, :, 0:CTX], tap(0), None, ALU.mult))
                    for j in range(1, 4):
                        ins = nc.vector.scalar_tensor_tensor(out=dst, in0=src[:, :, j:j + CTX], scalar=tap(j), in1=dst,
                                                             op0=ALU.mult, op1=ALU.add)
                        if j < 3:
                            link(ins)
                    ins.then_inc(conv_done, 1)
                for e in norm_parts(n):
                    if e < 2 * GH:
                        tile, width = norm_tile(e)
                        wait_evacuated(dve, ("ksum", e))
                        nc.vector.scalar_tensor_tensor(out=tile, in0=tile, scalar=1.0 if e < GH else GDN_SCALE,
                                                       in1=gdn_sq[:, e % 2, 0:width], op0=ALU.mult,
                                                       op1=ALU.mult).then_inc(normed, 1)

            dve.wait_ge(gate_ready, 1)
            dve.wait_ge(levels_ready, 1)

            by_dir = lambda ap: ap.rearrange("p (d h) n -> p d h n", d=2)
            for job in [job for p in range(HEAD_PAIRS + 1) for job in core_steps(p)]:
                kind, p, c = job[0], job[1], job[-1]
                if kind in ("Z", "TT", "VN"):
                    continue
                if kind == "osum":
                    read_head(p)
                    continue
                wait_product(dve, job)
                if kind == "R":
                    for unit in range(4):
                        last = nc.vector.tensor_scalar(u_of(p, c)[:, unit, :], units(bank(job))[:, unit, :],
                                                       gate_cols(cum_g, c, unit, p), 0.0, ALU.subtract, ALU.min)
                    last.then_inc(diffs_ready, 1)
                elif kind == "G":
                    g = units(bank(job))
                    wait_evacuated(dve, ("R", p, c))
                    for d in range(2):
                        nc.vector.tensor_copy(wl[:, p % 2, c, 2 * d:2 * d + 2], u_of(p, c)[:, 2 * d:2 * d + 2, end_col(d)])
                    if c >= LAT_CHUNK:
                        for d in range(2):
                            pair = slice(2 * d, 2 * d + 2)
                            last = nc.vector.tensor_tensor(attn_of(p, c - LAT_CHUNK, pair), g[:, 2:4, :],
                                                           u_of(p, c)[:, pair, :], ALU.mult)
                        last.then_inc(attn_raw, 1)
                    for unit in range(4):
                        last = nc.vector.scalar_tensor_tensor(
                            out=n_mat[c][:, unit, :], in0=g[:, unit % 2, :], scalar=gate_cols(beta_g, c, unit, p),
                            in1=t_mat[c][:, unit, :], op0=ALU.mult, op1=ALU.mult)
                    release(last, job)
                elif kind in ("NT", "W"):
                    level = 0 if kind == "NT" else job[2]
                    release(nc.vector.tensor_tensor(by_dir(masked_w[:, c % 2]), by_dir(units(bank(job))),
                                                    both(level_mask[:, level, 1:3, :]), ALU.mult), job)
                    wait_evacuated(dve, job)
                    old = ident.unsqueeze(1).to_broadcast([P, 4, P]) if level == 0 else u_of(p, c)
                    nc.vector.tensor_tensor(u_of(p, c), old, masked_w[:, c % 2], ALU.subtract).then_inc(u_ready, 1)
                elif kind == "KS":
                    dve.wait_ge(vb_ready, p * CHUNKS + c + 1)
                    cc = [scan_chunk(unit // 2, c) for unit in range(4)]
                    for unit in range(4):
                        last = nc.vector.scalar_tensor_tensor(
                            out=scan_rhs[:, unit, :], in0=bank(job)[:, unit * P:(unit + 1) * P],
                            scalar=gate_cols(neg_decay, cc[unit], unit, p), in1=v_beta[:, c % 2, unit, :],
                            op0=ALU.mult, op1=ALU.add)
                    release(last, job)
                elif kind == "S" and c == 0:
                    release(nc.vector.tensor_copy(state, units(bank(job))), job)
                elif kind == "S":
                    cc = [scan_chunk(unit // 2, c) for unit in range(4)]
                    for unit in range(4):
                        last = nc.vector.scalar_tensor_tensor(
                            out=state[:, unit, :], in0=state[:, unit, :], scalar=el[:, p % 2, cc[unit], unit:unit + 1],
                            in1=bank(job)[:, unit * P:(unit + 1) * P], op0=ALU.mult, op1=ALU.add)
                    release(last, job)
                else:
                    if c > LAT_CHUNK:
                        wait_evacuated(dve, ("O", p, c - 1))
                    for d in range(2):
                        at_ = (scan_chunk(d, c) - LAT_CHUNK) * CHUNK
                        dst = o_fm[:, 2 * p:2 * p + 2, at_:at_ + CHUNK]
                        src = units(bank(job))[:, 2 * d:2 * d + 2, :]
                        if c == LAT_CHUNK:
                            last = nc.vector.tensor_copy(dst, src)
                        else:
                            last = nc.vector.tensor_tensor(dst, dst, src, ALU.add)
                    release(last, job)

            split_to(where[("gdnout", 0)] + 2)
            for h in readout_heads(HEAD_PAIRS + 1):
                read_head(h)

        def gdn_gpsimd(pool, link, split_o):
            pool.wait_ge(x_updated, 2 * KT)
            for n in range(2):
                nc.gpsimd.memset(conv_in[n][:, :, 0:2], 0.0)
                last = nc.gpsimd.memset(conv_in[n][:, :, CTX + 2:CTX + 3], 0.0)
            last.then_inc(pads_ready, 1)
            def split_head(h):
                pool.wait_ge(o_hi_ready, KT + h + 1)
                split_o(h, read_t[:, h % 2, :], CTX)

            def scale_values(p, s):
                for unit in range(4):
                    last = nc.gpsimd.tensor_scalar(v_beta[:, s % 2, unit, :],
                                                   v_tok[:, scan_chunk(unit // 2, s), 2 * p + unit % 2, :],
                                                   gate_cols(beta_g, scan_chunk(unit // 2, s), unit, p), one,
                                                   ALU.mult, ALU.mult)
                last.then_inc(vb_ready, 1)

            for p in range(HEAD_PAIRS + 1):
                for c in range(CHUNKS if p < HEAD_PAIRS else 0):
                    if p:
                        wait_product(pool, ("Z", p - 1, LEVELS - 1, c))
                    elif c == 0:
                        wait_product(pool, ("gdn", "z", GH - 1))
                    for unit in range(4):
                        last = nc.gpsimd.tensor_scalar(n_mat[c][:, unit, :], tri[unit // 2],
                                                       gate_cols(log_decay, c, unit, p), one, ALU.mult, ALU.mult)
                    last.then_inc(tri_gates, 1)
                if p == 0:
                    for s in range(2):
                        scale_values(0, s)
                for kind, q, *rest in core_steps(p):
                    c = rest[-1] if rest else None
                    if kind == "G" and c >= LAT_CHUNK:
                        lat = slice((c - LAT_CHUNK) * CHUNK, (c - LAT_CHUNK + 1) * CHUNK)
                        wait_evacuated(pool, ("R", p, c))
                        if p == 0:
                            pool.wait_ge(normed, 2 * GH)
                        for d in range(2):
                            nc.gpsimd.tensor_tensor(q_dec_of(p, c - LAT_CHUNK, slice(2 * d, 2 * d + 2)),
                                                    q_fm[:, 2 * p:2 * p + 2, lat],
                                                    row_decay[:, c - LAT_CHUNK, 2 * d:2 * d + 2, :], ALU.mult)
                        pool.wait_ge(attn_raw, p * (CHUNKS - LAT_CHUNK) + c - LAT_CHUNK + 1)
                        for d in range(2):
                            part = attn_of(p, c - LAT_CHUNK, slice(2 * d, 2 * d + 2))
                            last = nc.gpsimd.tensor_tensor(part, part, tri[d].unsqueeze(1).to_broadcast([P, 2, P]),
                                                           ALU.mult)
                        last.then_inc(attn_ready, 1)
                    if kind == "VN" and c == 0:
                        wait_product(pool, ("VN", q, 0))
                        scale_values(q, 2)
                    if kind == "KS" and (c == 1 or q + 1 < HEAD_PAIRS):
                        wait_evacuated(pool, ("KS", q, c))
                        scale_values(*((q, 3) if c == 1 else (q + 1, c - 2)))
                    if kind == "osum":
                        split_head(q)
            for h in readout_heads(HEAD_PAIRS + 1):
                split_head(h)

        block = stack.enter_context(nc.Block())

        @block.tensor
        def _(pe):
            jobs = [0]

            def finish(ins, job):
                jobs[0] += 1
                done_at[job] = jobs[0]
                ins.then_inc(products_done, 1)

            def take(job, ring="work"):
                b = RINGS[ring][taken[ring] % len(RINGS[ring])]
                taken[ring] += 1
                if used[b]:
                    pe.wait_ge(evacuated[b], used[b])
                used[b] += 1
                turn_of[job] = (b, used[b])
                return banks[b]

            def turn_rows(group):
                pe.wait_ge(rows_ready, group + 1)
                dst = take(("mod", group))
                for k in range(ADA_WIDTH // P):
                    m = nc.tensor.matmul(dst[:, 2 * k:2 * k + 2], ada_rows[0:4, k * P:(k + 1) * P],
                                         tab[0:4, C_FOLD:C_FOLD + 2], start=True, stop=True)
                finish(m, ("mod", group))

            def ada(ids):
                for n in ids:
                    if n == 0:
                        pe.wait_ge(silu_split_ready, 1)
                    before, after = ada_turns(n)
                    for group in before:
                        turn_rows(group)
                    w = weights(("ada", n))
                    for t in range(ADA_TILES):
                        k = n % ADA_ROUNDS * ADA_TILES + t
                        nc.tensor.matmul(banks[0][0:4, :], silu_split[:, k, :], w(0, t), start=(k == 0), stop=False)
                        m = nc.tensor.matmul(banks[0][0:2, :], silu_split[:, k, 0:2], w(1, t), start=False,
                                             stop=(k == KT - 1))
                    finish(m, ("ada", n))
                    for group in after:
                        turn_rows(group)

            def three(dst, stationary, moving, kk, first, last, before=None):
                for k in kk:
                    if before:
                        before(k)
                    for a, b in ((0, 0), (0, 1), (1, 0)):
                        m = nc.tensor.matmul(dst, stationary(a, k), moving(b, k),
                                             start=(first and k == kk[0] and a == b == 0),
                                             stop=(last and k == kk[-1] and a == 1))
                return m

            def weights(key):
                n = where[key]
                pe.wait_ge(w_hi_ready, n + 1)
                pe.wait_ge(w_lo_ready, n + 1)
                slot = (w_hi[n % N_SPLIT], w_lo[n % N_RAW])
                if key[0] == "ada":
                    slot = [ap.rearrange("p (t a) m -> p t (a m)", t=ADA_TILES) for ap in slot]
                return lambda part, k: slot[part][:, k, :]

            def h_waits(i):
                return None if i is None else (lambda k: pe.wait_ge(h_ready, i * KT + k + 1))

            def project(key, job, lo, first_of=None, width=P):
                dst = take(job)[0:width, lo:T]
                w = weights(key)
                m = three(dst, lambda part, k: w(part, k)[:, 0:width], lambda part, k: (h_hi, h_lo)[part][:, k, lo:T],
                          range(KT), True, True, before=h_waits(first_of))
                finish(m, job)

            def to_tokens(job, src):
                width = src.shape[0]
                dst = take(job)
                for t in range(T // P):
                    m = nc.tensor.transpose(dst[:, t * width:(t + 1) * width], src[:, t * P:(t + 1) * P],
                                            ident[0:width, 0:width])
                finish(m, job)

            def pre_norm(i):
                lo = first_token(i)
                dst = take(("pre", i), "side")
                for k in range(KT):
                    pe.wait_ge(pre_sq_ready, i * KT + k + 1)
                    m = nc.tensor.matmul(dst[:, lo:T], ones, pre_sq[:, k % 4, lo:T],
                                         start=(k == 0), stop=(k == KT - 1))
                    finish(m, ("pre_sq", i, k))
                done_at[("pre", i)] = jobs[0]

            def post_norm(i):
                lo = first_out(i)
                pe.wait_ge(y_acc_ready, (i + 1) * KT)
                dst = take(("post", i), "side")
                finish(nc.tensor.matmul(dst[:, lo:T], ones, post_views[i][2][:, lo:T],
                                        start=True, stop=True), ("post", i))

            def out_project(i, name, base):
                for m in range(KT):
                    if m == 0:
                        pe.wait_ge(o_hi_ready, base)
                        pe.wait_ge(o_lo_ready, base)
                    project((name, m), ("y", i, m), first_out(i))

            def ffn(layer):
                i = 2 * layer + 1
                lo = first_token(i)
                for n in range(2 * FT):
                    project(("gate", layer, n), ("gate", layer, n), lo, i if n == 0 else None)
                    ada(ada_after(f"gate{layer}", n))
                for m in range(KT):
                    dst = take(("y", i, m))[:, lo:T]
                    for part, (a, b) in enumerate(DOWN_PARTS):
                        w = weights(("down", layer, m, part))

                        def hidden_there(k):
                            pe.wait_ge(act_hi_ready, layer * FT + k + 1)
                            pe.wait_ge(act_lo_ready, layer * FT + k + 1)
                        last = three(dst, lambda p, k: w(p, k - a),
                                     lambda p, k: (act_hi, act_lo)[p][:, k, lo:T], range(a, b),
                                     part == 0, part == 2, before=hidden_there if m == 0 else None)
                        finish(last, ("down", layer, m, part))
                    done_at[("y", i, m)] = jobs[0]
                    ada(ada_after(f"down{layer}", m))

            pe.wait_ge(tables_in, 16)
            pe.wait_ge(rows_in, 16 * ROW_DMAS)
            for n, (rows, count) in enumerate(((rowsA, R_N), (rowsB, 2 * 6 * KT), (rowsC, 4 * 3 * GH))):
                dst = take(("cols", n))
                finish(nc.tensor.transpose(dst[:, 0:count], rows[0:count, :], ident[0:count, 0:count]),
                       ("cols", n))
            ada(ada_after("start", 0)[:N_RAW])
            pe.wait_ge(tok_in, 16 * 2)
            for k in range(KT):
                dst = take(("x", k))
                for t in range(4):
                    m = nc.tensor.transpose(dst[:, t * P:(t + 1) * P], tok[:, t, k * P:(k + 1) * P], ident)
                finish(m, ("x", k))
            pre_norm(0)
            ada(ada_after("start", 0)[N_RAW:])

            for n in range(len(QKV_STEPS) + 2):
                if n < len(QKV_STEPS):
                    key = ("qkv",) + QKV_STEPS[n]
                    project(key, key, 0, 0 if n == 0 else None)
                    ada(ada_after("qkv", n))
                if 0 < n <= len(QKV_STEPS) and QKV_STEPS[n - 1] in V_TILES:
                    step = QKV_STEPS[n - 1]
                    wait_evacuated(pe, ("qkv",) + step)
                    to_tokens(("v_turned",) + step, v_fm[:, V_TILES.index(step) % 2, :])
                for u in stat_at(n):
                    wait_evacuated(pe, ("qkv",) + QK_TILES[u])
                    finish(nc.tensor.matmul(take(("qk_stat", u), "side"), block_ones, qk_sq[:, u % 2, :],
                                            start=True, stop=True), ("qk_stat", u))
                for u in rotate_at(n):
                    if u in NORMED:
                        pe.wait_ge(qk_normed, NORMED.index(u) + 1)
                    else:
                        wait_evacuated(pe, ("qkv",) + QK_TILES[u])
                    dst = take(("rot", u))
                    finish(nc.tensor.matmul(dst[:, 0:LAT], rotation, qk_n[:, u % 3, CTX:T],
                                            start=True, stop=True), ("rot", u))

            def scores(n):
                head, qb = ATT_UNITS[n]
                for m, (qt, half, kt) in enumerate(maps_of(head)):
                    if qb == 0:
                        pe.wait_ge(qk_out, 5 + qt + 1)
                    dst = take(("s", n, m))
                    finish(nc.tensor.matmul(dst[:, 0:keys_of(qb)], q_sb[:, qt, half, qb * P:(qb + 1) * P],
                                            k_sb[:, kt, 0:keys_of(qb)], start=True, stop=True), ("s", n, m))

            def turn(n):
                qb = ATT_UNITS[n][1]
                pe.wait_ge(probs_ready, n + 1)
                dst = take(("t", n))
                for t in range(keys_of(qb) // P):
                    m = nc.tensor.transpose(dst[:, t * P:(t + 1) * P],
                                            probs[:, n % 3, 0, t * P:(t + 1) * P], ident)
                finish(m, ("t", n))

            def values(n):
                head, qb = ATT_UNITS[n]
                if n == 0:
                    wait_evacuated(pe, ("v_turned", "dv", 3))
                if qb == 0:
                    take(("o", head), "side")
                dst = bank(("o", head))
                wait_evacuated(pe, ("t", n))
                c0 = head * P if head < DIFF_HEADS else 512 + (head - DIFF_HEADS) // 4 * P
                tiles = keys_of(qb) // P
                for t in range(tiles):
                    m = nc.tensor.matmul(dst[:, qb * P:(qb + 1) * P], v_sb[:, t, c0:c0 + P],
                                         probsT[:, n % 2, t, :], start=(t == 0), stop=(t == tiles - 1))
                finish(m, ("v", n))
                done_at[("o", head)] = jobs[0]

            for n in range(len(ATT_UNITS) + 4):
                if n < len(ATT_UNITS):
                    scores(n)
                    ada(ada_after("att", n))
                if 2 <= n < len(ATT_UNITS) + 2:
                    turn(n - 2)
                if 3 <= n < len(ATT_UNITS) + 3:
                    values(n - 3)
                if n in SUBLN_AT:
                    h = SUBLN_AT.index(n)
                    wait_evacuated(pe, ("o", h))
                    finish(nc.tensor.matmul(take(("o_stat", h)), ones, o_sq, start=True, stop=True),
                           ("o_stat", h))
            out_project(0, "attout", KT)
            post_norm(0)
            pre_norm(1)
            ffn(0)
            post_norm(1)
            if LAST_SUB == 3:
                pre_norm(2)
                gdn_tensor(pe, take, finish, project, to_tokens)
                out_project(2, "gdnout", 2 * KT)
                post_norm(2)
                pre_norm(3)
                ffn(1)
                post_norm(3)
            for half in range(2):
                for t in range(LAT // P):
                    dst = take(("out", t, half))
                    for k in range(4):
                        pe.wait_ge(x_updated, LAST_SUB * KT + 4 * half + k + 1)
                        m = nc.tensor.transpose(dst[:, k * P:(k + 1) * P],
                                                xT[:, 4 * half + k, CTX + t * P:CTX + (t + 1) * P], ident)
                    finish(m, ("out", t, half))

        @block.scalar
        def _(act):
            chain = [0]
            splits = [0]

            def link(ins):
                chain[0] += 1
                ins.then_inc(act_chain, 1)
                act.wait_ge(act_chain, chain[0])

            def split_to(n):
                while splits[0] <= min(n, len(chunks) - 1):
                    m = splits[0]
                    key = chunks[m]
                    if m >= N_SPLIT:
                        wait_product(act, split_job(chunks[m - N_SPLIT]))
                    wait_raw(act, key)
                    tiles, w = chunk_shape(key)
                    nc.scalar.activation(w_hi[m % N_SPLIT][:, 0:tiles, 0:w], raw_slot(key)[:, 0:tiles, 0:w],
                                         ACT.Copy).then_inc(w_hi_ready, 1)
                    splits[0] += 1

            def preload_logs():
                nc.scalar.preload_act_table_set("natural_log_exp_and_others")

            def rstd(dst, src, job, scale):
                wait_product(act, job)
                link(nc.scalar.activation(dst, src, ACT.Ln, bias=eps, scale=scale))
                release(nc.scalar.activation(dst, dst, ACT.Exp, scale=-0.5), job)

            def pre_norm(i):
                lo = first_token(i)
                layer, part = i // 2, 3 * (i % 2)
                if i:
                    split_to(where[FIRST_CHUNK[i]] + 2)
                for k in range(KT):
                    x_ready(act, i, k)
                    if k >= 4:
                        wait_product(act, ("pre_sq", i, k - 4))
                    nc.scalar.activation(pre_sq[:, k % 4, lo:T], xT[:, k, lo:T],
                                         ACT.Square).then_inc(pre_sq_ready, 1)
                rstd(pre_rstd[:, lo:T], bank(("pre", i))[:, lo:T], ("pre", i), 1.0 / D)
                split_to(where[FIRST_CHUNK[i]] + 2)
                act.wait_ge(mods_ready, layer * 4 + (3 if part else 1))
                for k in range(KT):
                    wait_scaled(act, "pre", i, k)
                    for s in range(lo // CTX, 2):
                        a, b = STREAMS[s]
                        last = nc.scalar.activation(h_work[:, k, a:b], h_work[:, k, a:b],
                                                    ACT.Identity, scale=mod_col(layer, part + 1, k, s),
                                                    bias=mod_col(layer, part, k, s))
                    last.then_inc(h32_ready, 1)

            def take_y(i, m):
                lo = first_out(i)
                wait_product(act, ("y", i, m))
                if m >= 2:
                    act.wait_ge(y_acc_ready, i * KT + m - 1)
                nc.scalar.activation(post_views[i][1][:, m % 2, lo:T], bank(("y", i, m))[:, lo:T], ACT.Square)
                release(nc.scalar.activation(y_views[i][:, m, lo:T], bank(("y", i, m))[:, lo:T], ACT.Copy),
                        ("y", i, m))

            def post_norm(i):
                lo = first_out(i)
                rstd(post_views[i][0][:, lo:T], bank(("post", i))[:, lo:T], ("post", i), 1.0 / D)

            def out_project(i, name):
                for m in range(KT):
                    split_to(where[(name, m)] + 2)
                    take_y(i, m)

            def ffn(layer):
                i = 2 * layer + 1
                lo = first_token(i)
                for n in range(2 * FT):
                    key = ("gate", layer, n)
                    j = layer * FT + n // 2
                    split_to(where[key] + 2)
                    if n % 2 == 0:
                        wait_product(act, key)
                        if n >= 4:
                            wait_evacuated(act, ("gate", layer, n - 3))
                        release(nc.scalar.activation(s_tmp[:, j % 2, lo:T], bank(key)[:, lo:T], ACT.Silu), key)
                    else:
                        wait_evacuated(act, key)
                        nc.scalar.activation(act_hi[:, n // 2, lo:T], a_tmp[:, j % 2, lo:T],
                                             ACT.Copy).then_inc(act_hi_ready, 1)
                preload_logs()
                for m in range(KT):
                    split_to(where[("down", layer, m, 2)] + 2)
                    take_y(i, m)

            wait_evacuated(act, ("cols", 0))
            nc.scalar.activation(silu_c, colsA[:, R_C:R_C + 2 * KT].rearrange("p (s k) -> p k s", s=2),
                                 ACT.Silu).then_inc(silu_ready, 1)
            act.wait_ge(silu_ready, 1)
            nc.scalar.activation(silu_split[:, :, 0:2], silu_c, ACT.Copy).then_inc(silu_ready, 1)
            preload_logs()
            act.wait_ge(lam_sums, 1)
            nc.scalar.activation(lam_two[:, 2:4], lam_two[:, 0:2], ACT.Exp).then_inc(lam_exps, 1)
            split_to(N_RAW - 1)
            pre_norm(0)
            for n in range(len(QKV_STEPS) + 2):
                if n < len(QKV_STEPS):
                    key = ("qkv",) + QKV_STEPS[n]
                    split_to(where[key] + 2)
                    if QKV_STEPS[n] in QK_TILES:
                        u = QK_TILES.index(QKV_STEPS[n])
                        wait_product(act, key)
                        if u >= 3:
                            act.wait_ge(qk_out, u - 2)
                        if u in NORMED:
                            if u - 2 in NORMED:
                                act.wait_ge(qk_normed, NORMED.index(u - 2) + 1)
                            nc.scalar.activation(qk_sq[:, u % 2, :], bank(key), ACT.Square)
                        release(nc.scalar.activation(qk_n[:, u % 3, :], bank(key), ACT.Copy), key)
                    else:
                        v = V_TILES.index(QKV_STEPS[n])
                        wait_product(act, key)
                        if v >= 2:
                            wait_product(act, ("v_turned",) + V_TILES[v - 2])
                        release(nc.scalar.activation(v_fm[:, v % 2, :], bank(key), ACT.Copy), key)
                for u in stat_at(n):
                    rstd(qk_sq[:, u % 2, :], bank(("qk_stat", u)), ("qk_stat", u), 1.0 / HEAD)

            for n in range(len(ATT_UNITS) + 4):
                for a in ada_after("att", n):
                    split_to(where[("ada", a)] + 2)
                if n < len(ATT_UNITS):
                    head, qb = ATT_UNITS[n]
                    for m in range(len(maps_of(head))):
                        act.wait_ge(max_ready, map_no(n, m) + 1)
                        if n >= 3:
                            wait_product(act, ("t", n - 3))
                        release(nc.scalar.activation(probs[:, n % 3, m, 0:keys_of(qb)],
                                                     bank(("s", n, m))[:, 0:keys_of(qb)], ACT.Exp,
                                                     bias=stats[:, n % 4, m:m + 1],
                                                     accum_out=stats[:, n % 4, 2 + m:3 + m]), ("s", n, m))
                if 3 <= n < len(ATT_UNITS) + 3 and ATT_UNITS[n - 3][1] == 3:
                    head = ATT_UNITS[n - 3][0]
                    src = bank(("o", head))
                    wait_product(act, ("o", head))
                    if head == 0:
                        act.wait_ge(qk_out, len(QK_TILES))
                    if head < DIFF_HEADS:
                        if head:
                            act.wait_ge(o_scaled, head)
                        nc.scalar.activation(o_sq, src, ACT.Square)
                        release(nc.scalar.activation(o_sb[:, head, :], src, ACT.Copy), ("o", head))
                    else:
                        tile, half = divmod(head - DIFF_HEADS, 2)
                        rows = slice(half * HEAD, (half + 1) * HEAD)
                        release(nc.scalar.activation(o_sb[rows, DIFF_HEADS + tile, :], src[rows, :], ACT.Copy),
                                ("o", head))
                if 2 <= n < len(ATT_UNITS) + 2:
                    keys = keys_of(ATT_UNITS[n - 2][1])
                    wait_product(act, ("t", n - 2))
                    if n >= 4:
                        wait_product(act, ("v", n - 4))
                    release(nc.scalar.activation(probsT[:, (n - 2) % 2, 0:keys // P, :],
                                                 units(bank(("t", n - 2))[:, 0:keys]), ACT.Copy), ("t", n - 2))
                if n in SUBLN_AT:
                    h = SUBLN_AT.index(n)
                    rstd(o_sq, bank(("o_stat", h)), ("o_stat", h), 1.0 / P)
            out_project(0, "attout")
            post_norm(0)
            pre_norm(1)
            ffn(0)
            post_norm(1)
            if LAST_SUB == 3:
                pre_norm(2)
                gdn_scalar(act, link, split_to, rstd, preload_logs)
                out_project(2, "gdnout")
                post_norm(2)
                pre_norm(3)
                ffn(1)
                post_norm(3)

        @block.vector
        def _(dve):
            chain = [0]
            splits = [0]

            def link(ins):
                chain[0] += 1
                ins.then_inc(dve_chain, 1)
                dve.wait_ge(dve_chain, chain[0])

            def split_to(n):
                while splits[0] <= min(n, len(chunks) - 1):
                    m = splits[0]
                    key = chunks[m]
                    tiles, w = chunk_shape(key)
                    dve.wait_ge(w_hi_ready, m + 1)
                    nc.vector.tensor_tensor(w_lo[where[key] % N_RAW][:, 0:tiles, 0:w], raw_slot(key)[:, 0:tiles, 0:w],
                                            w_hi[m % N_SPLIT][:, 0:tiles, 0:w].bitcast(F32),
                                            ALU.subtract).then_inc(w_lo_ready, 1)
                    splits[0] += 1

            def take_mods(group):
                layer, g = divmod(group, ADA_GROUPS)
                part, half = divmod(g, 2)
                job, tiles = ("mod", group), ADA_WIDTH // P
                wait_product(dve, job)
                col = (layer * 6 + part) * KT + half * tiles
                release(nc.vector.tensor_tensor(mods[:, layer, part, half * tiles:(half + 1) * tiles, :],
                                                bank(job)[:, 0:2 * tiles].rearrange("p (k s) -> p k s", s=2),
                                                ada_bias[:, col:col + tiles].unsqueeze(2).to_broadcast([P, tiles, 2]),
                                                ALU.add), job)
                if part % 3 and half:
                    dst = mods[:, layer, part, :, :]
                    wait_evacuated(dve, job)
                    g = R_NORM + (layer * 4 + (part // 3) * 2 + part % 3 - 1) * KT
                    gain = colsA[:, g:g + KT].unsqueeze(2).to_broadcast([P, KT, 2])
                    nc.vector.scalar_tensor_tensor(out=dst, in0=dst, scalar=float(part % 3 == 1), in1=gain,
                                                   op0=ALU.add, op1=ALU.mult).then_inc(mods_ready, 1)

            def ada(ids):
                for n in ids:
                    before, after = ada_turns(n)
                    for group in before:
                        take_mods(group)
                    if n % ADA_ROUNDS == ADA_ROUNDS - 1:
                        wait_product(dve, ("ada", n))
                        if n >= ADA_ROUNDS:
                            wait_product(dve, ("mod", n // ADA_ROUNDS - 1))
                        nc.vector.tensor_copy(ada_rows[0:4, :], banks[0][0:4, :]).then_inc(rows_ready, 1)
                    for group in after:
                        take_mods(group)

            def pre_norm(i):
                lo = first_token(i)
                if i:
                    split_to(where[FIRST_CHUNK[i]] + 2)
                for k in range(KT):
                    if (k + 1) in SCALED_BY_VECTOR["pre"]:
                        scale_pre(dve, i, k + 1, True)
                    dve.wait_ge(h32_ready, i * KT + k + 1)
                    link(nc.vector.tensor_copy(h_hi[:, k, lo:T], h_work[:, k, lo:T]))
                    nc.vector.tensor_tensor(h_lo[:, k, lo:T], h_work[:, k, lo:T],
                                            h_hi[:, k, lo:T].bitcast(F32), ALU.subtract).then_inc(h_ready, 1)

            def sum_y(i, m):
                lo = first_out(i)
                acc, sq = post_views[i][2][:, lo:T], post_views[i][1][:, m % 2, lo:T]
                wait_evacuated(dve, ("y", i, m))
                if m == 0:
                    nc.vector.tensor_copy(acc, sq).then_inc(y_acc_ready, 1)
                else:
                    dve.wait_ge(y_acc_ready, i * KT + m)
                    nc.vector.tensor_tensor(acc, acc, sq, ALU.add).then_inc(y_acc_ready, 1)

            def post_norm(i):
                layer, part = i // 2, 3 * (i % 2) + 2
                dve.wait_ge(mods_ready, layer * 4 + (4 if i % 2 else 2))
                for k in range(KT):
                    if k + 1 in SCALED_BY_VECTOR["post"]:
                        scale_post(dve, i, k + 1, True)
                    wait_scaled(dve, "post", i, k)
                    for s in range(first_out(i) // CTX, 2):
                        a, b = STREAMS[s]
                        last = nc.vector.scalar_tensor_tensor(
                            out=xT[:, k, a:b], in0=y_views[i][:, k, a:b],
                            scalar=mod_col(layer, part, k, s), in1=xT[:, k, a:b], op0=ALU.mult, op1=ALU.add)
                    last.then_inc(x_updated, 1)

            def ffn(layer):
                i = 2 * layer + 1
                lo = first_token(i)
                for n in range(2 * FT):
                    split_to(where[("gate", layer, n)] + 2)
                    if n % 2:
                        j = layer * FT + n // 2
                        key = ("gate", layer, n)
                        wait_product(dve, key)
                        wait_evacuated(dve, ("gate", layer, n - 1))
                        if n >= 5:
                            dve.wait_ge(act_lo_ready, j - 1)
                        release(nc.vector.tensor_tensor(a_tmp[:, j % 2, lo:T], bank(key)[:, lo:T],
                                                        s_tmp[:, j % 2, lo:T], ALU.mult), key)
                    ada(ada_after(f"gate{layer}", n))
                for m in range(KT):
                    split_to(where[("down", layer, m, 2)] + 2)
                    sum_y(i, m)
                    ada(ada_after(f"down{layer}", m))

            for n, (cols, count) in enumerate(((colsA, R_N), (ada_bias, 2 * 6 * KT), (conv_cols, 4 * 3 * GH))):
                wait_product(dve, ("cols", n))
                release(nc.vector.tensor_copy(cols[:, 0:count], bank(("cols", n))[:, 0:count]), ("cols", n))
            lam_pairs = lam_row.rearrange("p (a b d) -> p a b d", a=2, b=2)
            link(nc.vector.tensor_tensor(lam_pairs[:, :, 0, :], lam_pairs[:, :, 0, :], lam_pairs[:, :, 1, :],
                                         ALU.mult))
            nc.vector.tensor_reduce(lam_two[:, 0:2], lam_pairs[:, :, 0, :], AXIS_X, ALU.add).then_inc(lam_sums, 1)
            dve.wait_ge(silu_ready, 2)
            nc.vector.tensor_tensor(silu_split[:, :, 2:4], silu_c, silu_split[:, :, 0:2].bitcast(F32),
                                    ALU.subtract).then_inc(silu_split_ready, 1)
            dve.wait_ge(lam_exps, 1)
            link(nc.vector.tensor_tensor(lam_two[:, 4:5], lam_two[:, 3:4], lam_two[:, 2:3], ALU.subtract))
            nc.vector.tensor_scalar(lam_two[:, 4:5], lam_two[:, 4:5], -LAM_INIT, None, ALU.add)
            nc.vector.tensor_scalar(sub_gain, colsA[:, R_SUB:R_SUB + 1], 1.0 - LAM_INIT, None,
                                    ALU.mult).then_inc(lam_ready, 1)
            for n in ada_after("start", 0):
                split_to(where[("ada", n)] + 2 if n >= N_RAW else min(n + 2, N_RAW - 1))
                ada([n])
                if n == N_RAW - 1:
                    for k in range(KT):
                        wait_product(dve, ("x", k))
                        release(nc.vector.tensor_copy(xT[:, k, :], bank(("x", k))), ("x", k))
            pre_norm(0)

            for n in range(len(QKV_STEPS) + 2):
                if n == LEVELS_STEP:
                    dve.wait_ge(levels_in, 16)
                    nc.vector.tensor_copy(level_mask.rearrange("p a b c -> p (a b c)"),
                                          level_f32).then_inc(levels_ready, 1)
                if n < len(QKV_STEPS):
                    kind, t = QKV_STEPS[n]
                    split_to(where[("qkv", kind, t)] + 2)
                    ada(ada_after("qkv", n))
                if 0 < n <= len(QKV_STEPS) and QKV_STEPS[n - 1] in V_TILES:
                    kind, t = QKV_STEPS[n - 1]
                    job = ("v_turned", kind, t)
                    wait_product(dve, job)
                    src = units(bank(job))
                    if kind == "dv":
                        release(nc.vector.tensor_copy(v_sb[:, :, t * P:(t + 1) * P], src), job)
                    else:
                        dst = v_sb[:, :, 512:768].rearrange("p t (g r d) -> p t g r d", g=GQA_KV, r=2)
                        src = src.rearrange("p t (g d) -> p t g d", g=GQA_KV)
                        nc.vector.tensor_copy(dst[:, :, :, 0, :], src)
                        release(nc.vector.tensor_copy(dst[:, :, :, 1, :], src), job)
                for u in stat_at(n):
                    wait_evacuated(dve, ("qk_stat", u))
                    gain = colsA[:, R_QKG + (0 if QK_TILES[u][0] == "gq" else 1):][:, 0:1]
                    nc.vector.scalar_tensor_tensor(out=qk_n[:, u % 3, :], in0=qk_n[:, u % 3, :], scalar=gain,
                                                   in1=qk_sq[:, u % 2, :], op0=ALU.mult,
                                                   op1=ALU.mult).then_inc(qk_normed, 1)
                for u in rotate_at(n):
                    wait_product(dve, ("rot", u))
                    if u >= 2:
                        dve.wait_ge(qk_roped, u - 1)
                    release(nc.vector.tensor_tensor(qk_sined[:, u % 2, :], bank(("rot", u))[:, 0:LAT], sinT,
                                                    ALU.mult), ("rot", u))
                    wait_evacuated(dve, ("rot", u))
                    dve.wait_ge(qk_cos, u + 1)
                    nc.vector.tensor_tensor(qk_n[:, u % 3, CTX:T], qk_cosed[:, u % 2, :], qk_sined[:, u % 2, :],
                                            ALU.add).then_inc(qk_roped, 1)

            def maxima(n):
                head, qb = ATT_UNITS[n]
                for m in range(len(maps_of(head))):
                    wait_product(dve, ("s", n, m))
                    nc.vector.tensor_reduce(stats[:, n % 4, m:m + 1], bank(("s", n, m))[:, 0:keys_of(qb)], AXIS_X,
                                            ALU.max, negate=True).then_inc(max_ready, 1)

            def normalize(n):
                head, qb = ATT_UNITS[n]
                maps = len(maps_of(head))
                p = probs[:, n % 3, :, 0:keys_of(qb)]
                for m in range(maps):
                    wait_evacuated(dve, ("s", n, m))
                link(nc.vector.reciprocal(stats[:, n % 4, 4:4 + maps], stats[:, n % 4, 2:2 + maps]))
                first = nc.vector.tensor_scalar(p[:, 0, :], p[:, 0, :], stats[:, n % 4, 4:5], None, ALU.mult)
                if maps == 1:
                    first.then_inc(probs_ready, 1)
                    return
                link(first)
                if n == 0:
                    dve.wait_ge(lam_ready, 1)
                link(nc.vector.tensor_tensor(stats[:, n % 4, 5:6], stats[:, n % 4, 5:6], lam_two[:, 4:5], ALU.mult))
                nc.vector.scalar_tensor_tensor(out=p[:, 0, :], in0=p[:, 1, :], scalar=stats[:, n % 4, 5:6],
                                               in1=p[:, 0, :], op0=ALU.mult, op1=ALU.add).then_inc(probs_ready, 1)

            def split_o(tile):
                nc.vector.tensor_copy(h_hi[:, tile, :], o_sb[:, tile, :]).then_inc(o_hi_ready, 1)

            for n in range(len(ATT_UNITS) + 4):
                if n < len(ATT_UNITS):
                    maxima(n)
                    ada(ada_after("att", n))
                if 1 <= n < len(ATT_UNITS) + 1:
                    normalize(n - 1)
                for a in ada_after("att", n):
                    split_to(where[("ada", a)] + 2)
                if 3 <= n < len(ATT_UNITS) + 3 and ATT_UNITS[n - 3][1] == 3:
                    head = ATT_UNITS[n - 3][0]
                    if head >= DIFF_HEADS and head % 2:
                        wait_evacuated(dve, ("o", head - 1))
                        wait_evacuated(dve, ("o", head))
                        split_o(DIFF_HEADS + (head - DIFF_HEADS) // 2)
                if n in SUBLN_AT:
                    h = SUBLN_AT.index(n)
                    wait_evacuated(dve, ("o_stat", h))
                    nc.vector.scalar_tensor_tensor(out=o_sb[:, h, :], in0=o_sb[:, h, :], scalar=sub_gain,
                                                   in1=o_sq, op0=ALU.mult, op1=ALU.mult).then_inc(o_scaled, 1)
                    dve.wait_ge(o_scaled, h + 1)
                    split_o(h)
            for m in range(KT):
                split_to(where[("attout", m)] + 2)
                sum_y(0, m)
            post_norm(0)
            pre_norm(1)
            ffn(0)
            post_norm(1)
            if LAST_SUB == 3:
                pre_norm(2)
                gdn_vector(dve, link, split_to)
                for m in range(KT):
                    split_to(where[("gdnout", m)] + 2)
                    sum_y(2, m)
                post_norm(2)
                pre_norm(3)
                ffn(1)
                post_norm(3)
            for half in range(2):
                for t in range(LAT // P):
                    job = ("out", t, half)
                    wait_product(dve, job)
                    release(nc.vector.tensor_copy(out_sb[:, t, half * 512:(half + 1) * 512], bank(job)), job)

        @block.gpsimd
        def _(pool):
            chain = [0]

            def link(ins):
                chain[0] += 1
                ins.then_inc(pool_chain, 1)
                pool.wait_ge(pool_chain, chain[0])

            def pre_norm(i):
                for k in scaled_tiles("pre", False):
                    scale_pre(pool, i, k, False)

            def post_norm(i):
                for k in scaled_tiles("post", False):
                    scale_post(pool, i, k, False)

            def ffn(layer):
                lo = first_token(2 * layer + 1)
                for n in range(2 * FT):
                    if n % 2:
                        j = layer * FT + n // 2
                        pool.wait_ge(act_hi_ready, j + 1)
                        nc.gpsimd.tensor_tensor(act_lo[:, n // 2, lo:T], a_tmp[:, j % 2, lo:T],
                                                act_hi[:, n // 2, lo:T].bitcast(F32),
                                                ALU.subtract).then_inc(act_lo_ready, 1)

            def split_o(tile, src, lo):
                nc.gpsimd.tensor_tensor(h_lo[:, tile, lo:T], src, h_hi[:, tile, lo:T].bitcast(F32),
                                        ALU.subtract).then_inc(o_lo_ready, 1)

            pre_norm(0)
            for n in range(len(QKV_STEPS) + 2):
                for u in rotate_at(n):
                    if u in NORMED:
                        pool.wait_ge(qk_normed, NORMED.index(u) + 1)
                    else:
                        wait_evacuated(pool, ("qkv",) + QK_TILES[u])
                    if u >= 2:
                        pool.wait_ge(qk_roped, u - 1)
                    nc.gpsimd.tensor_tensor(qk_cosed[:, u % 2, :], qk_n[:, u % 3, CTX:T], cosT,
                                            ALU.mult).then_inc(qk_cos, 1)
                    pool.wait_ge(qk_roped, u + 1)
                    if u < 5:
                        last = nc.gpsimd.tensor_copy(k_sb[:, u, :], qk_n[:, u % 3, :])
                    else:
                        for half in range(2):
                            last = nc.gpsimd.tensor_scalar(q_sb[:, u - 5, half, :], qk_n[:, u % 3, :],
                                                           tab[:, C_HALF + half:C_HALF + half + 1], one,
                                                           ALU.mult, ALU.mult)
                    last.then_inc(qk_out, 1)
            for tile in range(KT):
                pool.wait_ge(o_hi_ready, tile + 1)
                split_o(tile, o_sb[:, tile, :], 0)
            post_norm(0)
            pre_norm(1)
            ffn(0)
            post_norm(1)
            if LAST_SUB == 3:
                pre_norm(2)
                gdn_gpsimd(pool, link, split_o)
                post_norm(2)
                pre_norm(3)
                ffn(1)
                post_norm(3)

        @block.sync
        def _(sp):
            def columns(w, lo, width=P):
                return w[:, lo:lo + width].rearrange("(k p) m -> p k m", p=P)

            def source(key):
                kind = key[0]
                if kind == "ada":
                    layer, n = divmod(key[1], ADA_GROUPS * ADA_ROUNDS)
                    group, part = divmod(n, ADA_ROUNDS)
                    rows = slice(part * ADA_TILES * P, (part + 1) * ADA_TILES * P)
                    return columns(ada_w[layer][rows, :], group * ADA_WIDTH, ADA_WIDTH)
                if kind == "qkv":
                    col = {"gk": GK_COL, "gv": GV_COL, "dk": DK_COL, "dv": DV_COL, "dq": DQ_COL}
                    return columns(attn_w_in[0], col[key[1]] + key[2] * P)
                if kind == "attout":
                    return columns(attn_w_out[0], key[1] * P)
                if kind == "gate":
                    j, up = divmod(key[2], 2)
                    return columns(ffn_w_gate_up[key[1]], up * FFN + j * P)
                if kind == "down":
                    a, b = DOWN_PARTS[key[3]]
                    return columns(ffn_w_down[key[1]][a * P:b * P, :], key[2] * P)
                if kind == "gdn":
                    col = {"q": 0, "k": GW, "v": 2 * GW, "z": 3 * GW, "ab": 4 * GW}[key[1]]
                    return columns(gdn_w_in[0], col + key[2] * P, chunk_shape(key)[1])
                return columns(gdn_w_out[0], key[1] * P)

            vec = lambda a, n: a.rearrange("(r p) -> r p", p=P)
            sp.dma_start(tab, tables).then_inc(tables_in, 16)
            row_dmas = [
                (rowsA[R_NORM:R_NORM + 64, :], norm_g.rearrange("l n (k p) -> (l n k) p", p=P)),
                (rowsA[R_C:R_C + 8, :], c_ctx.rearrange("(k p) -> k p", p=P)),
                (rowsA[R_C + 8:R_C + 16, :], c.rearrange("b (k p) -> (b k) p", p=P)),
                (rowsA[R_SUB:R_SUB + 1, :], diff_subln_g),
                (rowsA[R_GDN:R_GDN + 1, :], gdn_norm_g),
                (rowsA[R_QKG:R_QKG + 2, 0:HEAD], gqa_qk_g[0]),
                (rowsA[R_QKG:R_QKG + 2, HEAD:P], gqa_qk_g[0]),
                (rowsB[0:2 * 6 * KT, :], ada_b.rearrange("l (k p) -> (l k) p", p=P)),
                (rowsC[0:4 * 3 * GH, :], gdn_conv_w[0].rearrange("j (k p) -> (j k) p", p=P)),
                (lam_row, diff_lambda[0].rearrange("a d -> (a d)").partition_broadcast(P)),
                (dt_row, gdn_dt_bias[0].rearrange("a d -> (a d)").partition_broadcast(P)),
                (alog_row, gdn_a_log[0].rearrange("a d -> (a d)").partition_broadcast(P)),
            ]
            assert len(row_dmas) == ROW_DMAS
            for dst, src in row_dmas:
                sp.dma_start(dst, src).then_inc(rows_in, 16)
            for n, key in enumerate(chunks):
                if n == N_RAW:
                    sp.dma_start(tok[:, 0:2, :], ctx[0].rearrange("(t p) d -> p t d", p=P)).then_inc(tok_in, 16)
                    sp.dma_start(tok[:, 2:4, :], x[0].rearrange("(t p) d -> p t d", p=P)).then_inc(tok_in, 16)
                if key == ("qkv",) + QKV_STEPS[1]:
                    sp.dma_start(level_f32, levels).then_inc(levels_in, 16)
                if n >= N_RAW:
                    last = chunks[n - N_RAW]
                    wait_product(sp, split_job(last))
                slot, done = w_raw[n % N_RAW], raw_in[n % N_RAW]
                if key[:2] == ("qkv", "gq"):
                    for g in range(GQA_KV):
                        col = GQ_COL + g * (GQA_HEADS // GQA_KV) * HEAD + key[2] * HEAD
                        sp.dma_start(slot[:, :, g * HEAD:(g + 1) * HEAD],
                                     columns(attn_w_in[0], col, HEAD)).then_inc(done, 16)
                else:
                    src = source(key)
                    dst = slot.rearrange("p (t a) m -> p t (a m)", t=ADA_TILES) if key[0] == "ada" else slot
                    sp.dma_start(dst[:, 0:src.shape[1], 0:src.shape[2]], src).then_inc(done, 16)
            for t in range(LAT // P):
                for half in range(2):
                    wait_evacuated(sp, ("out", t, half))
                sp.dma_start(out[0, t * P:(t + 1) * P, :], out_sb[:, t, :]).then_inc(out_stored, 16)
            sp.wait_ge(out_stored, 16 * (LAT // P))


ROW_DMAS = 12
LAST_SUB = 3
LEVELS_STEP = 4
SUBLN_AT = [4 * h + 7 for h in range(DIFF_HEADS)]


def split_job(key):
    if key[0] in ("ada", "gate", "down", "qkv", "gdn"):
        return key
    return ("y", 0 if key[0] == "attout" else 2, key[1])


_INS = ['x', 'c', 'ctx', 'c_ctx', 'ada_w', 'ada_b', 'norm_g', 'attn_w_in', 'attn_w_out', 'diff_lambda',
        'diff_subln_g', 'gqa_qk_g', 'gdn_w_in', 'gdn_conv_w', 'gdn_a_log', 'gdn_dt_bias', 'gdn_norm_g',
        'gdn_w_out', 'ffn_w_gate_up', 'ffn_w_down']


def kernel(**inputs):
    import numpy as _np
    import concourse.bacc as _bacc
    from concourse import mybir as _mybir
    from concourse.bass_utils import run_bass_kernel_spmd as _run

    nc = _bacc.Bacc("TRN2", target_bir_lowering=False, num_devices=1)
    arrays, args = {}, []
    given = [(name, _np.ascontiguousarray(inputs[name])) for name in _INS]
    for name, a in given + [("tables", shape_tables()), ("levels", level_tables())]:
        arrays[f"in_{name}"] = a
        args.append(nc.dram_tensor(f"in_{name}", a.shape, _mybir.dt.from_np(a.dtype), kind="ExternalInput").ap())
    args.append(nc.dram_tensor("out_0", (1, LAT, D), F32, kind="ExternalOutput").ap())
    backbone(nc, *args)
    r = _run(nc, [arrays], core_ids=[0])
    return r.results[0]["out_0"]
```
